# Optimizing a Trainium2 kernel written in Bass

```python
import math
import jax, jax.numpy as jnp
from jax import lax
import numpy as np

D_MODEL = 1024
BATCH = 1
SEQ = 256
DEPTH = 2

N_META = 16
N_A = DEPTH // 2
N_B = DEPTH - N_A
N_HEADS = 8
HEAD_DIM = D_MODEL // N_HEADS
D_FF = 2816
CONV_WIDTH = 3
BLOCK = 128
PAD = (-N_META) % BLOCK
LN_EPS = 1e-5
DEEPNORM_ALPHA = (2 * DEPTH) ** 0.25
DEEPNORM_BETA = (8 * DEPTH) ** -0.25
NEG_INF = -1e30


def layer_norm(x, g, b):
    xf = x.astype(jnp.float32)
    mu = jnp.mean(xf, axis=-1, keepdims=True)
    var = jnp.mean(jnp.square(xf - mu), axis=-1, keepdims=True)
    y = (xf - mu) * lax.rsqrt(var + LN_EPS) * g.astype(jnp.float32) + b.astype(jnp.float32)
    return y.astype(x.dtype)

def swiglu(x, wg, wu, wd):
    return (jax.nn.silu(x @ wg) * (x @ wu)) @ wd

def short_conv(x, w_in, w_conv, w_out):
    bgate, cgate, val = jnp.split(x @ w_in, 3, axis=-1)
    u = cgate * val
    y = lax.conv_general_dilated(
        u, w_conv[:, None, :].astype(u.dtype),
        window_strides=(1,), padding=[(CONV_WIDTH - 1, 0)],
        dimension_numbers=("NWC", "WIO", "NWC"),
        feature_group_count=D_MODEL)
    return (bgate * y) @ w_out

def shared_kv(h, kv_w, f_bias):
    bsz, L, _ = h.shape
    kvf = h @ kv_w
    k = kvf[..., :D_MODEL].reshape(bsz, L, N_HEADS, HEAD_DIM)
    v = kvf[..., D_MODEL:2 * D_MODEL].reshape(bsz, L, N_HEADS, HEAD_DIM)
    f_logit = (kvf[..., 2 * D_MODEL:] + f_bias).astype(jnp.float32)
    log_f = jax.nn.log_sigmoid(f_logit)
    pad4 = ((0, 0), (PAD, 0), (0, 0), (0, 0))
    k = jnp.pad(k, pad4).transpose(0, 2, 1, 3)
    v = jnp.pad(v, pad4).transpose(0, 2, 1, 3)
    log_f = jnp.pad(log_f, ((0, 0), (PAD, 0), (0, 0)))
    c = jnp.cumsum(log_f, axis=1).transpose(0, 2, 1)
    return k, v, c

def forgetting_attention(h, w_q, w_o, k, v, c):
    bsz, L, _ = h.shape
    Lp = L + PAD
    n_blocks = Lp // BLOCK
    scale = 1.0 / math.sqrt(HEAD_DIM)
    q = (h @ w_q).reshape(bsz, L, N_HEADS, HEAD_DIM)
    q = jnp.pad(q, ((0, 0), (PAD, 0), (0, 0), (0, 0))).transpose(0, 2, 1, 3)
    k_pos = jnp.arange(Lp)

    def one_block(i):
        start = i * BLOCK
        qb = lax.dynamic_slice_in_dim(q, start, BLOCK, axis=2)
        cq = lax.dynamic_slice_in_dim(c, start, BLOCK, axis=2)
        s = jnp.einsum("bhqd,bhkd->bhqk", qb, k).astype(jnp.float32) * scale
        s = s + cq[..., :, None] - c[..., None, :]
        q_pos = start + jnp.arange(BLOCK)
        mask = (k_pos[None, :] <= q_pos[:, None]) & (k_pos[None, :] >= PAD)
        s = jnp.where(mask, s, NEG_INF)
        p = jax.nn.softmax(s, axis=-1)
        return jnp.einsum("bhqk,bhkd->bhqd", p.astype(v.dtype), v)

    o = lax.map(one_block, jnp.arange(n_blocks))
    o = o.transpose(1, 0, 3, 2, 4).reshape(bsz, Lp, D_MODEL)[:, PAD:]
    return o @ w_o

def first_inputs(seed: int = 0) -> dict:
    key = jax.random.key(seed)
    ks = jax.random.split(key, 20)
    f32 = jnp.float32

    def nrm(k, shape, scale):
        return jax.random.normal(k, shape, f32) * scale

    d_s = D_MODEL ** -0.5
    f_s = D_FF ** -0.5
    x = nrm(ks[0], (BATCH, SEQ, D_MODEL), 1.0)
    meta = nrm(ks[1], (N_META, D_MODEL), 1.0)
    ffn1_wg = nrm(ks[2], (DEPTH, D_MODEL, D_FF), d_s)
    ffn1_wu = nrm(ks[3], (DEPTH, D_MODEL, D_FF), d_s)
    ffn1_wd = nrm(ks[4], (DEPTH, D_FF, D_MODEL), f_s * DEEPNORM_BETA)
    ffn2_wg = nrm(ks[5], (DEPTH, D_MODEL, D_FF), d_s)
    ffn2_wu = nrm(ks[6], (DEPTH, D_MODEL, D_FF), d_s)
    ffn2_wd = nrm(ks[7], (DEPTH, D_FF, D_MODEL), f_s * DEEPNORM_BETA)
    ln_gain = 1.0 + nrm(ks[8], (DEPTH, 3, D_MODEL), 0.02)
    ln_bias = nrm(ks[9], (DEPTH, 3, D_MODEL), 0.02)
    conv_w_in = nrm(ks[10], (N_A, D_MODEL, 3 * D_MODEL), d_s)
    conv_w = nrm(ks[11], (N_A, CONV_WIDTH, D_MODEL), CONV_WIDTH ** -0.5)
    conv_w_out = nrm(ks[12], (N_A, D_MODEL, D_MODEL), d_s * DEEPNORM_BETA)
    w_k = nrm(ks[13], (D_MODEL, D_MODEL), d_s)
    w_v = nrm(ks[14], (D_MODEL, D_MODEL), d_s * DEEPNORM_BETA)
    w_f = nrm(ks[15], (D_MODEL, N_HEADS), d_s * 0.5)
    kv_w = jnp.concatenate([w_k, w_v, w_f], axis=1)
    f_bias = 3.0 + nrm(ks[16], (N_HEADS,), 0.5)
    attn_w_q = nrm(ks[17], (N_B, D_MODEL, D_MODEL), d_s)
    attn_w_o = nrm(ks[18], (N_B, D_MODEL, D_MODEL), d_s * DEEPNORM_BETA)
    return {"x": x, "meta": meta,
            "ffn1_wg": ffn1_wg, "ffn1_wu": ffn1_wu, "ffn1_wd": ffn1_wd,
            "ffn2_wg": ffn2_wg, "ffn2_wu": ffn2_wu, "ffn2_wd": ffn2_wd,
            "ln_gain": ln_gain, "ln_bias": ln_bias,
            "conv_w_in": conv_w_in, "conv_w": conv_w, "conv_w_out": conv_w_out,
            "kv_w": kv_w, "f_bias": f_bias,
            "attn_w_q": attn_w_q, "attn_w_o": attn_w_o}

def first_block(x, meta, ffn1_wg, ffn1_wu, ffn1_wd, ffn2_wg, ffn2_wu, ffn2_wd,
              ln_gain, ln_bias, conv_w_in, conv_w, conv_w_out, kv_w, f_bias,
              attn_w_q, attn_w_o):
    bsz = x.shape[0]
    h = jnp.concatenate(
        [jnp.broadcast_to(meta.astype(x.dtype)[None], (bsz, N_META, D_MODEL)), x], axis=1)
    k_sh = v_sh = c_sh = None
    for l in range(DEPTH):
        h = layer_norm(DEEPNORM_ALPHA * h + 0.5 * swiglu(h, ffn1_wg[l], ffn1_wu[l], ffn1_wd[l]),
                       ln_gain[l, 0], ln_bias[l, 0])
        if l < N_A:
            mix = short_conv(h, conv_w_in[l], conv_w[l], conv_w_out[l])
        else:
            j = l - N_A
            mix = forgetting_attention(h, attn_w_q[j], attn_w_o[j], k_sh, v_sh, c_sh)
        h = layer_norm(DEEPNORM_ALPHA * h + mix, ln_gain[l, 1], ln_bias[l, 1])
        h = layer_norm(DEEPNORM_ALPHA * h + 0.5 * swiglu(h, ffn2_wg[l], ffn2_wu[l], ffn2_wd[l]),
                       ln_gain[l, 2], ln_bias[l, 2])
        if l == N_A - 1:
            k_sh, v_sh, c_sh = shared_kv(h, kv_w, f_bias)
    return h[:, N_META:]


DEPTH_2 = 1

PAD_2 = BLOCK - N_META
EPS = 1e-6
NEG = -1e30
SSD_INNER = 2 * D_MODEL
SSD_HEADDIM = 64
SSD_HEADS = SSD_INNER // SSD_HEADDIM
SSD_GROUPS = 4
SSD_HPG = SSD_HEADS // SSD_GROUPS
SSD_STATE = 128
SSD_CONV = 4
SSD_XBC = SSD_INNER + 2 * SSD_GROUPS * SSD_STATE
ATT_HEADS = 16
ATT_KV_HEADS = 2
ATT_HEADDIM = 64
ATT_GQ = ATT_HEADS // ATT_KV_HEADS
WINDOW = 128
ATT_Q = ATT_HEADS * ATT_HEADDIM
ATT_KV = ATT_KV_HEADS * ATT_HEADDIM
REL_BUCKETS = 32
REL_MAX_DIST = 128
FFN_CONV = 3
N_BRANCH = 2
IN_WIDTHS = (SSD_INNER, SSD_XBC, SSD_HEADS, ATT_Q, ATT_KV, ATT_KV, D_MODEL, D_MODEL)
D_IN_PROJ = SSD_INNER + SSD_XBC + SSD_HEADS + ATT_Q + 2 * ATT_KV + N_BRANCH * D_MODEL


def rmsnorm(x, w):
    xf = x.astype(jnp.float32)
    y = xf * lax.rsqrt(jnp.mean(xf * xf, axis=-1, keepdims=True) + EPS)
    return (y * w.astype(jnp.float32)).astype(x.dtype)

def split_cols(t, widths):
    idx, acc = [], 0
    for w in widths[:-1]:
        acc += w
        idx.append(acc)
    return jnp.split(t, idx, axis=-1)

def causal_dwconv(x, w, b):
    k = w.shape[0]
    y = lax.conv_general_dilated(x, w[:, None, :].astype(x.dtype), window_strides=(1,),
                                 padding=[(k - 1, 0)], dimension_numbers=('NWC', 'WIO', 'NWC'),
                                 feature_group_count=x.shape[-1])
    return y + b.astype(x.dtype)

def t5_bucket(dist):
    max_exact = REL_BUCKETS // 2
    d = jnp.maximum(dist, 0)
    big = max_exact + (jnp.log(jnp.maximum(d, max_exact).astype(jnp.float32) / max_exact)
                       / math.log(REL_MAX_DIST / max_exact) * (REL_BUCKETS - max_exact)).astype(jnp.int32)
    return jnp.where(d < max_exact, d, jnp.minimum(big, REL_BUCKETS - 1))

def ssd_chunked(x, dt, a, bmat, cmat):
    bsz, lp = x.shape[:2]
    nc = lp // BLOCK
    f32 = jnp.float32
    xc = x.reshape(bsz, nc, BLOCK, SSD_GROUPS, SSD_HPG, SSD_HEADDIM).astype(f32)
    dtc = dt.reshape(bsz, nc, BLOCK, SSD_GROUPS, SSD_HPG)
    bc = bmat.reshape(bsz, nc, BLOCK, SSD_GROUPS, SSD_STATE).astype(f32)
    cc = cmat.reshape(bsz, nc, BLOCK, SSD_GROUPS, SSD_STATE).astype(f32)
    cs = jnp.cumsum(dtc * a.reshape(SSD_GROUPS, SSD_HPG), axis=2)
    xdt = xc * dtc[..., None]
    cs_t = jnp.moveaxis(cs, 2, -1)
    causal = jnp.tril(jnp.ones((BLOCK, BLOCK), dtype=bool))
    lmat = jnp.exp(jnp.where(causal, cs_t[..., :, None] - cs_t[..., None, :], -jnp.inf))
    cb = jnp.einsum('bclgn,bcsgn->bcgls', cc, bc)
    y_diag = jnp.einsum('bcgls,bcgrls,bcsgrp->bclgrp', cb, lmat, xdt)
    decay_states = jnp.exp(cs[:, :, -1:] - cs)
    states = jnp.einsum('bclgn,bclgr,bclgrp->bcgrpn', bc, decay_states, xdt)
    chunk_decay = jnp.exp(cs[:, :, -1])

    def step(hst, inp):
        st, dec = inp
        return dec[..., None, None] * hst + st, hst

    h0 = jnp.zeros((bsz, SSD_GROUPS, SSD_HPG, SSD_HEADDIM, SSD_STATE), f32)
    _, prev = lax.scan(step, h0, (jnp.moveaxis(states, 1, 0), jnp.moveaxis(chunk_decay, 1, 0)))
    prev = jnp.moveaxis(prev, 0, 1)
    y_off = jnp.einsum('bclgn,bcgrpn,bclgr->bclgrp', cc, prev, jnp.exp(cs))
    return (y_diag + y_off).reshape(bsz, lp, SSD_HEADS, SSD_HEADDIM)

def gated_group_rmsnorm(y, z, w):
    g = y * jax.nn.silu(z.astype(jnp.float32))
    gg = g.reshape(g.shape[:-1] + (SSD_GROUPS, SSD_INNER // SSD_GROUPS))
    gg = gg * lax.rsqrt(jnp.mean(gg * gg, axis=-1, keepdims=True) + EPS)
    return gg.reshape(g.shape) * w.astype(jnp.float32)

def swa_sink_attention(q, k, v, rel_bias, sinks):
    bsz, lp = q.shape[:2]
    nb = lp // BLOCK
    f32 = jnp.float32
    scale = ATT_HEADDIM ** -0.5
    qb = q.reshape(bsz, nb, BLOCK, ATT_KV_HEADS, ATT_GQ, ATT_HEADDIM)
    kb = k.reshape(bsz, nb, BLOCK, ATT_KV_HEADS, ATT_HEADDIM)
    vb = v.reshape(bsz, nb, BLOCK, ATT_KV_HEADS, ATT_HEADDIM)

    def with_prev(t):
        prev = jnp.pad(t, ((0, 0), (1, 0), (0, 0), (0, 0), (0, 0)))[:, :-1]
        return jnp.concatenate([prev, t], axis=2)

    kband, vband = with_prev(kb), with_prev(vb)
    pos = jnp.arange(lp, dtype=jnp.int32).reshape(nb, BLOCK)
    k_pos = jnp.concatenate([pos - BLOCK, pos], axis=1)
    dist = pos[:, :, None] - k_pos[:, None, :]
    mask_band = (k_pos[:, None, :] >= BLOCK) & (dist >= 0) & (dist < WINDOW)
    bias_band = rel_bias[t5_bucket(dist[0])].astype(f32)
    bias_band = jnp.transpose(bias_band, (2, 0, 1)).reshape(ATT_KV_HEADS, ATT_GQ, BLOCK, 2 * BLOCK)
    s_band = jnp.einsum('bnqkgd,bnskd->bnkgqs', qb, kband, preferred_element_type=f32) * scale + bias_band
    s_band = jnp.where(mask_band[None, :, None, None], s_band, NEG)
    meta_pos = PAD_2 + jnp.arange(N_META, dtype=jnp.int32)
    k_meta, v_meta = k[:, PAD_2:BLOCK], v[:, PAD_2:BLOCK]
    dist_m = pos[:, :, None] - meta_pos[None, None, :]
    bias_m = rel_bias[t5_bucket(dist_m)].astype(f32)
    bias_m = jnp.transpose(bias_m, (0, 3, 1, 2)).reshape(nb, ATT_KV_HEADS, ATT_GQ, BLOCK, N_META)
    s_meta = jnp.einsum('bnqkgd,bmkd->bnkgqm', qb, k_meta, preferred_element_type=f32) * scale + bias_m[None]
    s_meta = jnp.where((dist_m >= 0)[None, :, None, None], s_meta, NEG)
    sink = jnp.broadcast_to(sinks.astype(f32).reshape(1, 1, ATT_KV_HEADS, ATT_GQ, 1, 1),
                            s_meta.shape[:-1] + (1,))
    p = jax.nn.softmax(jnp.concatenate([s_meta, s_band, sink], axis=-1), axis=-1)
    p_meta = p[..., :N_META].astype(v.dtype)
    p_band = p[..., N_META:-1].astype(v.dtype)
    out = (jnp.einsum('bnkgqm,bmkd->bnqkgd', p_meta, v_meta)
           + jnp.einsum('bnkgqs,bnskd->bnqkgd', p_band, vband))
    return out.reshape(bsz, lp, ATT_Q)

def mixer_block(h, valid_f32, norm_w, w_in, conv_w, conv_b, dt_bias, a_log, d_skip, ssd_norm_w,
                w_ssd_branch, w_attn_branch, sinks, rel_bias, gate_b, w_out):
    bsz, lp = h.shape[:2]
    f32 = jnp.float32
    u = rmsnorm(h, norm_w)
    z, xbc, dt_raw, q, k, v, g_ssd, g_att = split_cols(u @ w_in.astype(u.dtype), IN_WIDTHS)
    xbc = jax.nn.silu(causal_dwconv(xbc, conv_w, conv_b))
    xs, bm, cm = split_cols(xbc, (SSD_INNER, SSD_GROUPS * SSD_STATE, SSD_GROUPS * SSD_STATE))
    dt = jax.nn.softplus(dt_raw.astype(f32) + dt_bias.astype(f32)) * valid_f32[None, :, None]
    a = -jnp.exp(a_log.astype(f32))
    xh = xs.reshape(bsz, lp, SSD_HEADS, SSD_HEADDIM)
    y = ssd_chunked(xh, dt, a, bm.reshape(bsz, lp, SSD_GROUPS, SSD_STATE),
                    cm.reshape(bsz, lp, SSD_GROUPS, SSD_STATE))
    y = y + d_skip.astype(f32)[:, None] * xh.astype(f32)
    y = gated_group_rmsnorm(y.reshape(bsz, lp, SSD_INNER), z, ssd_norm_w).astype(h.dtype)
    y_ssd = y @ w_ssd_branch.astype(h.dtype)
    att = swa_sink_attention(q.reshape(bsz, lp, ATT_HEADS, ATT_HEADDIM),
                             k.reshape(bsz, lp, ATT_KV_HEADS, ATT_HEADDIM),
                             v.reshape(bsz, lp, ATT_KV_HEADS, ATT_HEADDIM), rel_bias, sinks)
    y_att = att @ w_attn_branch.astype(h.dtype)
    gb = gate_b.astype(h.dtype)
    merged = jax.nn.sigmoid(g_ssd + gb[0]) * y_ssd + jax.nn.sigmoid(g_att + gb[1]) * y_att
    return merged @ w_out.astype(h.dtype)

def conv_ffn(h, norm_w, w_in, conv_w, conv_b, w_down):
    u = rmsnorm(h, norm_w)
    hid = causal_dwconv(u @ w_in.astype(u.dtype), conv_w, conv_b)
    up, gate = jnp.split(hid, 2, axis=-1)
    return (jax.nn.silu(gate) * up) @ w_down.astype(h.dtype)

def second_inputs(seed: int = 0) -> dict:
    key = jax.random.key(seed)
    ks = jax.random.split(key, 24)
    f32 = jnp.float32
    nrm = lambda k, shape, s: jax.random.normal(k, shape, f32) * s
    dt0 = jnp.exp(jax.random.uniform(ks[5], (DEPTH_2, SSD_HEADS), f32, math.log(1e-3), math.log(1e-1)))
    return {
        'x': nrm(ks[0], (BATCH, SEQ, D_MODEL), 1.0),
        'meta_tokens': nrm(ks[1], (N_META, D_MODEL), 1.0),
        'norm_mix_w': 1.0 + nrm(ks[2], (DEPTH_2, D_MODEL), 0.05),
        'w_in': nrm(ks[3], (DEPTH_2, D_MODEL, D_IN_PROJ), D_MODEL ** -0.5),
        'ssd_conv_w': nrm(ks[4], (DEPTH_2, SSD_CONV, SSD_XBC), SSD_CONV ** -0.5),
        'ssd_conv_b': nrm(ks[6], (DEPTH_2, SSD_XBC), 0.01),
        'ssd_dt_bias': dt0 + jnp.log(-jnp.expm1(-dt0)),
        'ssd_a_log': jnp.log(jax.random.uniform(ks[7], (DEPTH_2, SSD_HEADS), f32, 1.0, 16.0)),
        'ssd_d': 1.0 + nrm(ks[8], (DEPTH_2, SSD_HEADS), 0.1),
        'ssd_norm_w': 1.0 + nrm(ks[9], (DEPTH_2, SSD_INNER), 0.05),
        'w_ssd_branch': nrm(ks[10], (DEPTH_2, SSD_INNER, D_MODEL), SSD_INNER ** -0.5),
        'w_attn_branch': nrm(ks[11], (DEPTH_2, ATT_Q, D_MODEL), ATT_Q ** -0.5),
        'attn_sinks': nrm(ks[12], (DEPTH_2, ATT_HEADS), 0.5),
        'rel_bias': nrm(ks[13], (REL_BUCKETS, ATT_HEADS), 0.5),
        'gate_b': nrm(ks[14], (DEPTH_2, N_BRANCH, D_MODEL), 0.1),
        'w_out': nrm(ks[15], (DEPTH_2, D_MODEL, D_MODEL), D_MODEL ** -0.5),
        'norm_ffn_w': 1.0 + nrm(ks[16], (DEPTH_2, D_MODEL), 0.05),
        'w_ffn_in': nrm(ks[17], (DEPTH_2, D_MODEL, 2 * D_FF), D_MODEL ** -0.5),
        'ffn_conv_w': nrm(ks[18], (DEPTH_2, FFN_CONV, 2 * D_FF), FFN_CONV ** -0.5),
        'ffn_conv_b': nrm(ks[19], (DEPTH_2, 2 * D_FF), 0.01),
        'w_ffn_out': nrm(ks[20], (DEPTH_2, D_FF, D_MODEL), D_FF ** -0.5),
        'norm_final_w': 1.0 + nrm(ks[21], (D_MODEL,), 0.05),
    }

def second_block(x, meta_tokens, norm_mix_w, w_in, ssd_conv_w, ssd_conv_b, ssd_dt_bias, ssd_a_log, ssd_d,
              ssd_norm_w, w_ssd_branch, w_attn_branch, attn_sinks, rel_bias, gate_b, w_out, norm_ffn_w,
              w_ffn_in, ffn_conv_w, ffn_conv_b, w_ffn_out, norm_final_w):
    bsz, seq = x.shape[:2]
    lp = seq + BLOCK
    meta = jnp.broadcast_to(meta_tokens.astype(x.dtype)[None], (bsz, N_META, D_MODEL))
    h = jnp.concatenate([jnp.zeros((bsz, PAD_2, D_MODEL), x.dtype), meta, x], axis=1)
    valid = jnp.arange(lp) >= PAD_2
    valid_f32 = valid.astype(jnp.float32)
    valid_h = valid.astype(x.dtype)[None, :, None]
    for i in range(DEPTH_2):
        h = h + valid_h * mixer_block(h, valid_f32, norm_mix_w[i], w_in[i], ssd_conv_w[i], ssd_conv_b[i],
                                      ssd_dt_bias[i], ssd_a_log[i], ssd_d[i], ssd_norm_w[i], w_ssd_branch[i],
                                      w_attn_branch[i], attn_sinks[i], rel_bias, gate_b[i], w_out[i])
        h = h + valid_h * conv_ffn(h, norm_ffn_w[i], w_ffn_in[i], ffn_conv_w[i], ffn_conv_b[i], w_ffn_out[i])
    y = rmsnorm(h, norm_final_w)
    return y[:, BLOCK:]


def setup_inputs(seed=0):
    out = dict(first_inputs(seed))
    for name, value in second_inputs(seed + 1).items():
        if name != "x":
            out[name + "_2"] = value
    return out


def reference(
    x, meta, ffn1_wg, ffn1_wu, ffn1_wd, ffn2_wg, ffn2_wu, ffn2_wd, ln_gain, ln_bias, conv_w_in,
    conv_w, conv_w_out, kv_w, f_bias, attn_w_q, attn_w_o, meta_tokens_2, norm_mix_w_2, w_in_2,
    ssd_conv_w_2, ssd_conv_b_2, ssd_dt_bias_2, ssd_a_log_2, ssd_d_2, ssd_norm_w_2,
    w_ssd_branch_2, w_attn_branch_2, attn_sinks_2, rel_bias_2, gate_b_2, w_out_2, norm_ffn_w_2,
    w_ffn_in_2, ffn_conv_w_2, ffn_conv_b_2, w_ffn_out_2, norm_final_w_2,
):
    x = first_block(
        x, meta, ffn1_wg, ffn1_wu, ffn1_wd, ffn2_wg, ffn2_wu, ffn2_wd, ln_gain, ln_bias,
        conv_w_in, conv_w, conv_w_out, kv_w, f_bias, attn_w_q, attn_w_o,
    )
    return second_block(
        x, meta_tokens_2, norm_mix_w_2, w_in_2, ssd_conv_w_2, ssd_conv_b_2, ssd_dt_bias_2,
        ssd_a_log_2, ssd_d_2, ssd_norm_w_2, w_ssd_branch_2, w_attn_branch_2, attn_sinks_2,
        rel_bias_2, gate_b_2, w_out_2, norm_ffn_w_2, w_ffn_in_2, ffn_conv_w_2, ffn_conv_b_2,
        w_ffn_out_2, norm_final_w_2,
    )


_drawn_inputs = setup_inputs


def setup_inputs(seed=0):
    import zlib

    import numpy as np

    out = dict(_drawn_inputs(seed))
    spreads = {}
    factors = {'ssd_conv_b_2': 7.92, 'attn_sinks_2': 8.0, 'gate_b_2': 2.719, 'ffn_conv_b_2': 8.0}
    for name, (base, spread) in spreads.items():
        noise = np.random.default_rng([zlib.crc32(name.encode()), seed]).standard_normal(out[name].shape)
        drawn = base * np.exp(spread * noise) if base else spread * noise
        out[name] = __import__('jax').numpy.asarray(drawn.astype(out[name].dtype))
    for name, factor in factors.items():
        out[name] = (out[name] * factor).astype(out[name].dtype)
    return out
```

```python
import math
from contextlib import ExitStack

import numpy as np
import concourse.bass as bass
from concourse import mybir
from concourse.alu_op_type import AluOpType as ALU

F32 = mybir.dt.float32
F32R = mybir.dt.float32r
ACT = mybir.ActivationFunctionType
AX = mybir.AxisListType

T = 272
NMETA = 16
D = 1024
KD = 8
FF = 2816
KF = 22
ALPHA = 4 ** 0.25
QT = ((0, 16), (16, 144), (144, 272))
ST = ((0, 128), (128, 256), (256, 272))
TS = 14
NV = T - TS
NEG = -1e30
STRIP = 384
MSTRIP = 288


def constants():
    ident = np.eye(128, dtype=np.float32)
    causal = np.where(np.arange(128)[None, :] <= np.arange(128)[:, None], 0.0, NEG).astype(np.float32)
    cm = np.concatenate([np.zeros((128, 144), np.float32), causal], axis=1)
    tri = (np.arange(128)[None, :] >= np.arange(128)[:, None]).astype(np.float32)
    one = np.ones((128, 144), np.float32)
    t432 = np.concatenate([tri, one, tri, one[:, :16], tri[:, :16]], axis=1)

    def bucket(dist):
        d = np.maximum(dist, 0)
        big = 16 + (np.log(np.maximum(d, 16).astype(np.float32) / np.float32(16))
                    / np.float32(math.log(128 / 16)) * np.float32(16)).astype(np.int32)
        return np.where(d < 16, d, np.minimum(big, 31))

    db, dm = 255 - np.arange(STRIP), 271 - np.arange(MSTRIP)
    both = np.concatenate([db, dm])
    hot = (bucket(both)[None, :] == np.arange(32)[:, None]).astype(np.float32)
    ok = np.concatenate([(db >= 0) & (db < 128), dm >= 0])
    smask = np.broadcast_to(np.where(ok, 0.0, NEG).astype(np.float32), (16, both.size))
    return {"c_ident": ident, "c_cm": cm, "c_tri": t432, "c_hot": hot,
            "c_smask": np.ascontiguousarray(smask)}


class Queue:

    def __init__(self, sem):
        self.items, self.sem, self.n = [], sem, 0

    def wait(self, *tickets):
        for t in tickets:
            if t is None:
                continue
            if isinstance(t, list):
                self.wait(*t)
            else:
                self.items.append(("wait", t[0], t[1]))

    def quiet(self, fn, *after):
        self.wait(*after)
        self.items.append(("run", fn, None, 0))

    def do(self, fn, *after):
        self.wait(*after)
        self.n += 1
        self.items.append(("run", fn, self.sem, 1))
        return (self.sem, self.n)

    def dma(self, fn, sem, *after):
        self.wait(*after)
        self.items.append(("run", fn, sem, 16))

    def place(self):
        inner = Queue(None)
        self.items.append(("place", inner))
        return inner

    def run(self, eng, seen=None):
        seen = {} if seen is None else seen
        for it in self.items:
            if it[0] == "wait":
                if seen.get(id(it[1]), 0) < it[2]:
                    seen[id(it[1])] = it[2]
                    eng.wait_ge(it[1], it[2])
            elif it[0] == "place":
                it[1].run(eng, seen)
            else:
                ins = it[1](eng)
                if it[2] is not None:
                    ins.then_inc(it[2], it[3])


def program(nc, A, out, scratch):
    ctx = ExitStack()
    with ctx:
        build(nc, A, out, scratch, ctx)


def build(nc, A, out, scratch, ctx):
    uid = [0]

    def sb(stack, shape, dt=F32):
        uid[0] += 1
        return stack.enter_context(nc.sbuf_tensor(f"t{uid[0]}", shape, dt))

    def sem(name):
        return ctx.enter_context(nc.semaphore(name))

    PE, AC, DV, GP, SP = (Queue(sem(f"s_{n}")) for n in ("pe", "act", "dve", "pool", "sp"))

    NR, NH, LA = 4, 3, 2
    raw = [sb(ctx, [128, 2048]) for _ in range(NR)]
    wh = [sb(ctx, [128, 2048], F32R) for _ in range(NH)]
    wl = [sb(ctx, [128, 2048], F32R) for _ in range(NH)]
    H = sb(ctx, [128, KD, T])
    XH = sb(ctx, [128, KD, T], F32R)
    XL = sb(ctx, [128, KD, T], F32R)
    PV = sb(ctx, [128, 4, 128])
    ident = sb(ctx, [128, 128])
    identR = sb(ctx, [128, 128], F32R)
    mean1 = sb(ctx, [128, 128])
    mean5 = sb(ctx, [128, 128])
    cm = sb(ctx, [128, T])
    tri = sb(ctx, [128, 432])
    RS = sb(ctx, [128, T])
    LNV = sb(ctx, [128, T])
    cc = sb(ctx, [128, 4])
    PS = [ctx.enter_context(nc.psum_tensor(f"ps{i}", [128, 512], F32)) for i in range(8)]
    bank = [None] * 8

    s_c, s_x, s_p = sem("s_c"), sem("s_x"), sem("s_p")
    b1 = ExitStack()
    cstk = ExitStack()
    XC = sb(b1, [128, KD, T])
    prow = XC[:, 0:2, :].rearrange("p a c -> p (a c)")[:, 0:512].rearrange("p (a c) -> p a c", a=4)
    X0, X1, X2 = sb(cstk, [16, D]), sb(cstk, [128, D]), sb(cstk, [128, D])
    SP.dma(lambda e: e.dma_start(ident[:], A["c_ident"]), s_x)
    SP.dma(lambda e: e.dma_start(X0[:], A["meta"]), s_x)
    SP.dma(lambda e: e.dma_start(X1[:], A["x"][0, 0:128, :]), s_x)
    SP.dma(lambda e: e.dma_start(X2[:], A["x"][0, 128:256, :]), s_x)
    x_in = (s_x, 64)
    s_raw = [sem(f"s_raw{i}") for i in range(NR)]
    GP.wait((s_raw[0], 16))
    GP.dma(lambda e: e.dma_start(cm[:], A["c_cm"]), s_c)
    GP.dma(lambda e: e.dma_start(tri[:], A["c_tri"]), s_c)

    rows = [
        [("ln_gain", "l a (c p) -> (l a c) p"), ("ln_bias", "l a (c p) -> (l a c) p"),
         ("conv_w", "l k (c p) -> (l k c) p"), ("norm_mix_w_2", "l (c p) -> (l c) p")],
        [("ssd_conv_w_2", "l k (c p) -> (l k c) p"), ("ssd_conv_b_2", "l (c p) -> (l c) p"),
         ("norm_ffn_w_2", "l (c p) -> (l c) p")],
        [("ffn_conv_w_2", None), ("norm_final_w_2", "(c p) -> c p"),
         ("ssd_norm_w_2", "l (c p) -> (l c) p"), ("gate_b_2", "l a (c p) -> (l a c) p")],
        [("ffn_conv_w_2", None), ("ffn_conv_b_2", "l (c p) -> (l c) p")],
    ]
    col = {}
    nrow, n_p = [0] * 4, 0
    for t, parts in enumerate(rows):
        for name, how in parts:
            if how is None:
                v = A[name].rearrange("l k (c p) -> (l k c) p", p=128)
                v, key = (v[0:88], "fw01") if t == 2 else (v[88:132], "fw2")
            else:
                v, key = A[name].rearrange(how, p=128), name
            r0, n = nrow[t], v.shape[0]
            GP.dma(lambda e, t=t, r0=r0, n=n, v=v: e.dma_start(prow[r0:r0 + n, t, :], v), s_p)
            col[key] = (t, r0)
            nrow[t] += n
            n_p += 16

    def pc(key, i):
        t, r0 = col[key]
        return PV[:, t, r0 + i:r0 + i + 1]

    m_c = DV.do(lambda e: e.memset(mean1[:], 1.0 / 1024))
    DV.do(lambda e: e.memset(mean5[:], 1.0 / 512))
    DV.do(lambda e: e.memset(cc[:, 0:1], 1e-5))
    DV.do(lambda e: e.memset(cc[:, 1:2], 1e-6))
    m_c = DV.do(lambda e: e.memset(cc[:, 2:3], 1.0))
    t_idr = AC.do(lambda e: e.activation(identR[:], ident[:], ACT.Copy), x_in)

    s_wh, s_wl = sem("s_wh"), sem("s_wl")
    first = (AC.place(), DV.place())
    marks, unit_done = [], []
    side = []
    rate = [2]

    def unit(src, nk, ncol):
        n = len(unit_done)
        r, h, size = n % NR, n % NH, nk * ncol
        dst = raw[r][:, 0:size].rearrange("p (k c) -> p k c", k=nk)
        v = src.rearrange("(k p) c -> p k c", p=128)
        SP.dma(lambda e: e.dma_start(dst, v), s_raw[r], (s_wl, n - NR + 1) if n >= NR else None)
        loaded = (s_raw[r], 16 * (n // NR + 1))
        pa, pd = marks[n - LA] if n >= LA else first
        pa.wait(loaded, unit_done[n - NH] if n >= NH else None)
        pa.items.append(("run", lambda e: e.activation(wh[h][:, 0:size], raw[r][:, 0:size], ACT.Copy), s_wh, 1))
        pd.wait((s_wh, n + 1))
        pd.items.append(("run", lambda e: e.tensor_tensor(
            wl[h][:, 0:size], raw[r][:, 0:size], wh[h][:, 0:size].bitcast(F32), ALU.subtract), s_wl, 1))
        marks.append((AC.place(), DV.place()))
        unit_done.append(None)
        hi = wh[h][:, 0:size].rearrange("p (k c) -> p k c", k=nk)
        lo = wl[h][:, 0:size].rearrange("p (k c) -> p k c", k=nk)
        return n, hi, lo, (s_wl, n + 1)

    def run_side(n):
        while n > 0 and side:
            side.pop(0)()
            n -= 1

    def advance():
        if not side:
            credit[0] = 0.0
            return
        credit[0] += rate[0] / 8
        while credit[0] >= 1:
            credit[0] -= 1
            run_side(1)

    def drain():
        run_side(len(side) + 1000)

    pair, ring, credit = [0], [(0, 2)], [0.0]

    def gemm(src, nk, c0, nch, xs, n0, n1, evac):
        pair[0] = (pair[0] + 1) % len(ring[0])
        b0 = ring[0][pair[0]]
        N = n1 - n0
        tk = [None] * nch
        for kg in range(0, nk, 8):
            g = min(8, nk - kg)
            n, hi, lo, ready = unit(src[kg * 128:(kg + g) * 128, c0:c0 + 128 * nch], g, 128 * nch)
            if kg == 0:
                PE.wait(*[bank[b0 + m] for m in range(nch)])
            PE.wait(ready)
            for k in range(g):
                xh, xl, after = xs[kg + k]
                PE.wait(after)
                for m in range(nch):
                    o = PS[b0 + m][:, 0:N]
                    a, b = hi[:, k, m * 128:(m + 1) * 128], lo[:, k, m * 128:(m + 1) * 128]
                    xh_, xl_ = xh[:, n0:n1], xl[:, n0:n1]
                    st, sp = kg + k == 0, kg + k == nk - 1
                    PE.quiet(lambda e, o=o, a=a, x=xh_, st=st: e.matmul(o, a, x, start=st, stop=False))
                    PE.quiet(lambda e, o=o, a=a, x=xl_: e.matmul(o, a, x, start=False, stop=False))
                    last = lambda e, o=o, a=b, x=xh_, sp=sp: e.matmul(o, a, x, start=False, stop=sp)
                    if sp or (k == g - 1 and m == nch - 1):
                        tk[m] = unit_done[n] = PE.do(last)
                    else:
                        PE.quiet(last)
                if not (kg + k == nk - 1):
                    advance()
        free = evac([PS[b0 + m][:, 0:N] for m in range(nch)], tk)
        for m in range(nch):
            bank[b0 + m] = free[m]
        advance()

    def split(src, hi, lo, *after):
        a = AC.do(lambda e: e.activation(hi, src, ACT.Copy), *after)
        d = DV.do(lambda e: e.tensor_tensor(lo, src, hi.bitcast(F32), ALU.subtract), a, *after)
        return [a, d]

    def ptr(o, i, rows):
        return lambda e: e.transpose(o, i, ident[0:rows, 0:rows])

    def copy_act(o, i, scale=1.0):
        return lambda e: e.activation(o, i, ACT.Copy, scale=scale)

    def fn_act(o, i, f, **kw):
        return lambda e: e.activation(o, i, f, **kw)

    def tt(o, a, b, op):
        return lambda e: e.tensor_tensor(o, a, b, op)

    def stt(o, a, s, b, op0, op1):
        return lambda e: e.scalar_tensor_tensor(out=o, in0=a, scalar=s, in1=b, op0=op0, op1=op1)

    def ts(o, a, s1, s2, op0, op1=None):
        if op1 is None:
            return lambda e: e.tensor_scalar(o, a, s1, None, op0)
        return lambda e: e.tensor_scalar(o, a, s1, s2, op0, op1)

    def mm(o, a, b, st=True, sp=True):
        return lambda e: e.matmul(o, a, b, start=st, stop=sp)

    def now():
        return [(q.sem, q.n) for q in (PE, AC, DV, GP) if q.n]

    xs = []
    h_t = [None] * KD
    for c in range(KD):
        b = 4 + c % 4
        f = slice(c * 128, (c + 1) * 128)
        PE.quiet(ptr(PS[b][:, 0:16], X0[:, f], 16), x_in, bank[b])
        PE.quiet(ptr(PS[b][:, 16:144], X1[:, f], 128))
        t = PE.do(ptr(PS[b][:, 144:272], X2[:, f], 128))
        h_t[c] = DV.do(lambda e, c=c, b=b: e.tensor_copy(H[:, c, :], PS[b][:, 0:T]), t)
        s = split(PS[b][:, 0:T], XH[:, c, :], XL[:, c, :], h_t[c])
        bank[b] = s + [h_t[c]]
        xs.append((XH[:, c, :], XL[:, c, :], s))
    p_t = []
    prow_done = []

    def params(t):
        n = nrow[t]
        k = PE.do(ptr(PS[6][:, 0:n], prow[0:n, t, :], n), (s_p, n_p), bank[6])
        bank[6] = AC.do(copy_act(PV[:, t, 0:n], PS[6][:, 0:n]), k)
        p_t.append(bank[6])
        prow_done.append(k)
    for t in range(4):
        side.append(lambda t=t: params(t))
    fence = now()
    cstk.close()

    R = sb(b1, [128, KD, T])
    SQ = sb(b1, [128, 4, T])
    KXH = sb(b1, [128, KD, T], F32R)
    KXL = sb(b1, [128, KD, T], F32R)
    r_free = [list(fence) + [prow_done]]
    acc_t = [None]

    def residual(j, n0):
        def evac(ps, tk):
            free = []
            for m in range(2):
                k = 2 * j + m
                t = DV.do(stt(R[:, k, n0:T], H[:, k, n0:T], ALPHA, ps[m], ALU.mult, ALU.add),
                          tk[m], h_t[k], r_free[0])
                free.append(t)

            for k in (2 * j, 2 * j + 1):
                if k == 1:
                    acc_t[0] = DV.do(tt(LNV[:, n0:T], R[:, 0, n0:T], R[:, 1, n0:T], ALU.add), free)
                elif k > 1:
                    acc_t[0] = DV.do(tt(LNV[:, n0:T], LNV[:, n0:T], R[:, k, n0:T], ALU.add), free, acc_t[0])
            return free
        return evac

    def rstd(psum, tk, eps, n):
        a = AC.do(fn_act(LNV[:, 0:n], psum, ACT.Ln, bias=cc[:, eps:eps + 1]), tk, m_c)
        return a, AC.do(fn_act(RS[:, 0:n], LNV[:, 0:n], ACT.Exp, scale=-0.5), a)

    def layer_norm(i, hi, lo, n0=0):
        drain()
        sq_free = [None, None]
        var_t = None
        c_t = []
        warm = AC.do(fn_act(cc[:, 3:4], cc[:, 2:3], ACT.Ln), m_c)
        mean = PS[7][:, n0:T]
        mean_t = PE.do(mm(mean, mean1[:], LNV[:, n0:T]), acc_t[0], bank[7])
        for j in range(4):
            s = slice(2 * j, 2 * j + 2)
            m = mean.unsqueeze(1).to_broadcast([128, 2, T - n0])
            c_t.append(DV.do(tt(XC[:, s, n0:T], R[:, s, n0:T], m, ALU.subtract), mean_t, r_free[0]))
            q = slice(2 * (j % 2), 2 * (j % 2) + 2)
            a = AC.do(fn_act(SQ[:, q, n0:T], XC[:, s, n0:T], ACT.Square), c_t[j], sq_free[j % 2])
            for k in (2 * j, 2 * j + 1):
                f = mm(PS[6][:, n0:T], mean1[:], SQ[:, k % 4, n0:T], k == 0, k == KD - 1)
                var_t = PE.do(f, a, bank[6] if k == 0 else None)
            sq_free[j % 2] = var_t
        bank[7] = c_t[-1]
        a, r = rstd(PS[6][:, n0:T], var_t, 0, T - n0)
        bank[6] = a
        res, d = [], [None] * KD

        def scale(k):
            d[k] = DV.do(tt(XC[:, k, n0:T], XC[:, k, n0:T], RS[:, 0:T - n0], ALU.mult), r, c_t[k // 2])
        scale(0)
        scale(1)
        for k in range(KD):
            g, b = pc("ln_gain", 8 * i + k), pc("ln_bias", 8 * i + k)
            a1 = AC.do(fn_act(hi[:, k, n0:T], XC[:, k, n0:T], ACT.Identity, scale=g, bias=b), d[k], p_t)
            a2 = AC.do(fn_act(H[:, k, n0:T], XC[:, k, n0:T], ACT.Identity, scale=g, bias=b))
            h_t[k] = a2
            l = DV.do(tt(lo[:, k, n0:T], H[:, k, n0:T], hi[:, k, n0:T].bitcast(F32), ALU.subtract), a2)
            if k + 2 < KD:
                scale(k + 2)
            res.append((hi[:, k, :], lo[:, k, :], [a1, l]))
        r_free[0] = [c_t[-1], var_t, a2, l]
        return res

    def ffn(wg, wu, wd, xs, n0=0):
        with ExitStack() as st:
            fence = now()
            HH, HL = sb(st, [128, KF, T], F32R), sb(st, [128, KF, T], F32R)
            SG = [sb(st, [128, 2, T]) for _ in range(2)]
            hid = []
            sg_t, hp_free = [None, None], [fence, fence]
            ring[0] = (0, 2, 4)
            for j in range(11):
                s = j % 2

                def evac_g(ps, tk):
                    sg_t[s] = [AC.do(fn_act(SG[s][:, m, n0:T], ps[m], ACT.Silu), tk[m], hp_free[s]) for m in range(2)]
                    return sg_t[s]

                def evac_u(ps, tk):
                    free = [DV.do(stt(SG[s][:, m, n0:T], SG[s][:, m, n0:T], 0.5, ps[m], ALU.mult, ALU.mult),
                                  tk[m], sg_t[s][m]) for m in range(2)]
                    hs = [split(SG[s][:, m, n0:T], HH[:, 2 * j + m, n0:T], HL[:, 2 * j + m, n0:T], free[m], fence)
                          for m in range(2)]
                    hp_free[s] = hs[0] + hs[1]
                    hid.extend((HH[:, 2 * j + m, :], HL[:, 2 * j + m, :], hs[m]) for m in range(2))
                    return free
                gemm(wg, KD, 256 * j, 2, xs, n0, T, evac_g)
                gemm(wu, KD, 256 * j, 2, xs, n0, T, evac_u)
            drain()
            for j in range(4):
                gemm(wd, KF, 256 * j, 2, hid, n0, T, residual(j, n0))
            ring[0] = (0, 2)

    def short_conv(xs):
        with ExitStack() as st:
            fence = now()
            CH, CL = sb(st, [128, KD, T], F32R), sb(st, [128, KD, T], F32R)
            CT = [sb(st, [128, 2, T]) for _ in range(2)]
            Y = [sb(st, [128, 2, T]) for _ in range(2)]
            w_in = A["conv_w_in"][0]
            res = []
            u_free, y_free = [fence, fence], [fence, fence]
            ct, yt = [None], [None]
            for j in range(4):
                s = j % 2

                def evac_c(ps, tk):
                    ct[0] = [AC.do(copy_act(CT[s][:, m, :], ps[m]), tk[m], u_free[s]) for m in range(2)]
                    return ct[0]

                def evac_v(ps, tk):
                    u = [DV.do(tt(CT[s][:, m, :], CT[s][:, m, :], ps[m], ALU.mult), tk[m], ct[0][m]) for m in range(2)]
                    y = [DV.do(ts(Y[s][:, m, :], CT[s][:, m, :], pc("conv_w", 16 + 2 * j + m), None, ALU.mult),
                               u[m], p_t, y_free[s]) for m in range(2)]
                    for o in (1, 2):
                        y = [DV.do(stt(Y[s][:, m, o:T], CT[s][:, m, 0:T - o], pc("conv_w", 8 * (2 - o) + 2 * j + m),
                                       Y[s][:, m, o:T], ALU.mult, ALU.add), y[m]) for m in range(2)]
                    u_free[s] = y
                    yt[0] = y
                    return u

                def evac_b(ps, tk):
                    free = [DV.do(tt(Y[s][:, m, :], Y[s][:, m, :], ps[m], ALU.mult), tk[m], yt[0][m]) for m in range(2)]
                    hs = [split(Y[s][:, m, :], CH[:, 2 * j + m, :], CL[:, 2 * j + m, :], free[m], fence)
                          for m in range(2)]
                    y_free[s] = hs[0] + hs[1]
                    res.extend((CH[:, 2 * j + m, :], CL[:, 2 * j + m, :], hs[m]) for m in range(2))
                    return free
                gemm(w_in, KD, 1024 + 256 * j, 2, xs, 0, T, evac_c)
                gemm(w_in, KD, 2048 + 256 * j, 2, xs, 0, T, evac_v)
                gemm(w_in, KD, 256 * j, 2, xs, 0, T, evac_b)
            for j in range(4):
                gemm(A["conv_w_out"][0], KD, 256 * j, 2, res, 0, T, residual(j, 0))

    ffn(A["ffn1_wg"][0], A["ffn1_wu"][0], A["ffn1_wd"][0], xs)
    xs = layer_norm(0, XH, XL)
    short_conv(xs)
    xs = layer_norm(1, XH, XL)
    ffn(A["ffn2_wg"][0], A["ffn2_wu"][0], A["ffn2_wd"][0], xs)
    kxs = layer_norm(2, KXH, KXL)

    fg = ExitStack()
    NCF = sb(fg, [128, T])
    NCH, NCL = sb(fg, [128, T], F32R), sb(fg, [128, T], F32R)
    CTT = sb(fg, [128, 3, 8])
    FB = sb(fg, [8, 1])
    RB = sb(fg, [32, 16])
    xf = XC[:, :, :].rearrange("p a c -> p (a c)")
    rf = R[:, :, :].rearrange("p a c -> p (a c)")
    CB = [xf[:, 0:528], xf[:, 528:1056]]
    Z8, L8 = xf[0:8, 1056:1328], xf[0:8, 1328:1600]
    WF = xf[:, 1600:1664].rearrange("p (k c) -> p k c", k=KD)
    XM, SMK = rf[0:16, 0:1024], rf[0:16, 1024:1024 + STRIP + MSTRIP]
    HOT = SQ[0:32, :, :].rearrange("p a c -> p (a c)")[:, 0:STRIP + MSTRIP]
    s_f, s_b = sem("s_f"), sem("s_b")
    s_nc = []
    v = {}
    fence = now()
    GP.dma(lambda e: e.dma_start(WF, A["kv_w"][:, 2048:2056].rearrange("(k p) c -> p k c", p=128)), s_f, fence)
    GP.dma(lambda e: e.dma_start(FB[:], A["f_bias"].rearrange("(p a) -> p a", a=1)), s_f)
    GP.dma(lambda e: e.dma_start(XM, A["meta_tokens_2"]), s_f)
    GP.dma(lambda e: e.dma_start(RB[:], A["rel_bias_2"]), s_b)
    GP.dma(lambda e: e.dma_start(HOT, A["c_hot"]), s_b)
    GP.dma(lambda e: e.dma_start(SMK, A["c_smask"]), s_b)
    v["zero"] = [DV.do(lambda e, b=b: e.memset(b, 0.0), fence) for b in CB]

    def logits(k):
        v["t"] = PE.do(mm(PS[6][0:8, 0:T], WF[:, k, :], H[:, k, :], k == 0, k == KD - 1),
                       (s_f, 48), h_t[k], bank[6] if k == 0 else None)

    def logits_out():
        v["z"] = v["t"] = AC.do(fn_act(Z8, PS[6][0:8, 0:T], ACT.Identity, bias=FB[:, 0:1]), v["t"])
        bank[6] = v["z"]

    def softplus_steps(z, n, tmp, v):
        def s1():
            v["t"] = AC.do(fn_act(tmp, z, ACT.Abs), v["t"])

        def s2():
            v["t"] = AC.do(fn_act(tmp, tmp, ACT.Exp, scale=-1.0), v["t"])

        def s3():
            v["t"] = AC.do(fn_act(tmp, tmp, ACT.Ln, bias=cc[0:n, 2:3]), v["t"], m_c)
        return [s1, s2, s3]

    def log_gate():
        v["t"] = DV.do(stt(CB[0][0:8, 256:256 + T], Z8, 0.0, L8, ALU.min, ALU.subtract), v["t"], v["zero"])

    def cumsum_steps(bufs, n, v):
        def add(i, s):
            a, b = bufs[i], bufs[1 - i]
            v["t"] = DV.do(tt(b[0:n, 256:256 + T], a[0:n, 256:256 + T], a[0:n, 256 - s:256 - s + T], ALU.add), v["t"])
        return [lambda i=i: add(i % 2, 1 << i) for i in range(9)]
    C = CB[1][:, 256:256 + T]

    def gates_out():
        v["a"] = AC.do(fn_act(NCF[:], C, ACT.Copy, scale=-1.0), v["t"])

    def gates_split():
        s_nc.extend(split(NCF[:], NCH[:], NCL[:], v["a"]))

    def gates_T():
        for i, (q0, q1) in list(enumerate(QT))[1:]:
            k = PE.do(ptr(PS[6][0:q1 - q0, 8 * i:8 * i + 8], C[0:8, q0:q1], 8), v["t"], bank[6])
        bank[6] = AC.do(copy_act(CTT[:, 1:3, :], PS[6][:, 8:24].rearrange("p (a c) -> p a c", a=2)), k)
        s_nc.append(bank[6])

    def meta2():
        for k in range(KD):
            t = PE.do(ptr(PS[6][:, 16 * k:16 * k + 16], XM[:, k * 128:(k + 1) * 128], 16), (s_f, 48), bank[6])
        t = DV.do(lambda e: e.tensor_copy(H[:, :, 0:16], PS[6][:, 0:128].rearrange("p (k t) -> p k t", k=KD)),
                  t, v["z"])
        bank[6] = t
        h_t[:] = [[x, t] for x in h_t]
        r_free[0] = r_free[0] + [t] + s_nc

    WS = STRIP + MSTRIP
    sv = scratch

    def strips():
        k = PE.do(mm(PS[6][0:16, 0:STRIP], RB[:], HOT[:, 0:STRIP]), (s_b, 48), bank[6])
        k2 = PE.do(mm(PS[7][0:16, 0:MSTRIP], RB[:], HOT[:, STRIP:]), bank[7])
        d = DV.do(tt(SMK[:, 0:STRIP], SMK[:, 0:STRIP], PS[6][0:16, 0:STRIP], ALU.add), k)
        d2 = DV.do(tt(SMK[:, STRIP:], SMK[:, STRIP:], PS[7][0:16, 0:MSTRIP], ALU.add), k2)
        bank[6], bank[7] = d, d2
        GP.dma(lambda e: e.dma_start(sv.rearrange("q h j -> h q j"),
                                     SMK.unsqueeze(1).to_broadcast([16, 128, WS])), s_b, d, d2)
        r_free[0] = r_free[0] + [(s_b, 64)]
    side += [lambda k=k: logits(k) for k in range(KD)] + [logits_out]
    side += softplus_steps(Z8, 8, L8, v) + [log_gate] + cumsum_steps(CB, 8, v)
    side += [gates_out, gates_split, gates_T, meta2, strips]

    ffn(A["ffn1_wg"][1], A["ffn1_wu"][1], A["ffn1_wd"][1], kxs, NMETA)
    xs = layer_norm(3, XH, XL, NMETA)

    def zero_pad(bufs, fence):
        return [DV.do(lambda e, b=b: e.memset(b[:], 0.0), fence) for b in bufs]

    class Softmax:

        def __init__(self, st, fence, tiles):
            self.tiles = tiles
            self.SS = [sb(st, [128, 432]) for _ in range(2)]
            self.P = [sb(st, [128, 432]) for _ in range(2)]
            self.PT0 = [sb(st, [128, T]) for _ in range(1)]
            self.PT1 = [sb(st, [128, 256]) for _ in range(1)]
            self.PT2 = [sb(st, [128, 128]) for _ in range(1)]
            self.MX = [sb(st, [128, 3]) for _ in range(2)]
            self.NM = [sb(st, [128, 3]) for _ in range(2)]
            self.SM = [sb(st, [128, 3]) for _ in range(2)]
            self.RC = [sb(st, [128, 3]) for _ in range(2)]
            self.init = zero_pad(self.MX + self.SM + self.PT0, fence)
            self.fence = fence
            self.p_free, self.s_free, self.pt_free = [None] * 2, [None] * 2, None
            self.p_t, self.ex_t = [None] * 2, [None] * 2

        COLS = ((416, 432), (272, 416), (0, 272))

        def reduce_exp(self, i, s_t, sink=None):
            SS, P, MX, NM, SM = (x[i] for x in (self.SS, self.P, self.MX, self.NM, self.SM))
            mx = []
            for q in self.tiles:
                c0, c1 = self.COLS[q]
                n = 16 if q == 0 else 128
                mx.append(DV.do(lambda e, c0=c0, c1=c1, n=n, q=q: e.tensor_reduce(
                    MX[0:n, q:q + 1], SS[0:n, c0:c1], AX.X, ALU.max), s_t[q], self.init))
            if sink is None:
                nm = DV.do(ts(NM[:], MX[:], -1.0, None, ALU.mult), mx)
            else:
                nm = DV.do(ts(NM[:], MX[:], sink, -1.0, ALU.max, ALU.mult), mx)
            ex = []
            for q in self.tiles:
                c0, c1 = self.COLS[q]
                n = 16 if q == 0 else 128
                ex.append(AC.do(fn_act(P[0:n, c0:c1], SS[0:n, c0:c1], ACT.Exp, bias=NM[0:n, q:q + 1],
                                       accum_out=SM[0:n, q:q + 1]), nm, self.p_free[i], self.fence))
            self.s_free[i] = ex
            es = None
            if sink is not None:
                es = AC.do(fn_act(MX[:], NM[:], ACT.Exp, bias=sink), nm)
            self.ex_t[i] = ex, es

        def normalise(self, i):
            P, MX, SM, RC = (x[i] for x in (self.P, self.MX, self.SM, self.RC))
            ex, es = self.ex_t[i]
            if es is not None:
                ex = [DV.do(tt(SM[:], SM[:], MX[:], ALU.add), es, ex)]
            rc = [DV.do(lambda e: e.reciprocal(RC[:, 1:3], SM[:, 1:3]), ex)]
            if 0 in self.tiles:
                rc.append(DV.do(lambda e: e.reciprocal(RC[0:16, 0:1], SM[0:16, 0:1])))
            pt = []
            for q in self.tiles:
                c0, c1 = self.COLS[q]
                n = 16 if q == 0 else 128
                pt.append(DV.do(ts(P[0:n, c0:c1], P[0:n, c0:c1], RC[0:n, q:q + 1], None, ALU.mult), rc))
            self.p_t[i] = pt

        def transposes(self, i):
            P = self.P[i]
            PE.wait(self.p_t[i], bank[6], bank[7])
            t0 = 16
            if 0 in self.tiles:
                t0 = 0
                PE.quiet(ptr(PS[6][0:16, 0:16], P[0:16, 416:432], 16))
            PE.quiet(ptr(PS[6][0:16, 16:144], P[:, 272:288], 128))
            PE.quiet(ptr(PS[6][0:16, 144:272], P[:, 0:16], 128))
            k6 = PE.do(ptr(PS[6][:, 272:400], P[:, 144:272], 128))
            PE.quiet(ptr(PS[7][:, 0:128], P[:, 288:416], 128))
            k7 = PE.do(ptr(PS[7][:, 128:256], P[:, 16:144], 128))
            self.p_free[i] = k7
            a0 = AC.do(copy_act(self.PT0[0][0:16, t0:272], PS[6][0:16, t0:272]), k6, self.pt_free, self.init)
            a2 = AC.do(copy_act(self.PT2[0][:], PS[6][:, 272:400]), k6)
            a1 = DV.do(lambda e: e.tensor_copy(self.PT1[0][:], PS[7][:, 0:256]), k7, self.pt_free, self.fence)
            bank[6], bank[7] = a2, a1
            return [a0, a1, a2]

    with ExitStack() as st:
        fence = now()
        OH, OL = sb(st, [128, KD, T], F32R), sb(st, [128, KD, T], F32R)
        QF, KF_, VF = ([sb(st, [128, 2, T]) for _ in range(2)] for _ in range(3))
        VM = [sb(st, [128, 3, 128]) for _ in range(2)]
        sm = Softmax(st, fence, (2, 1))
        vm_init = zero_pad(VM, fence)
        heads = {}
        ores = [None] * 8
        qkv_free = [fence, fence]

        def step_a(h):
            p, m, i = (h // 2) % 2, h % 2, h % 2
            q, k, v = QF[p][:, m, :], KF_[p][:, m, :], VF[p][:, m, :]
            inq = heads[h // 2]
            e_r = identR[:, h:h + 1].to_broadcast([128, 128])
            PE.wait(inq, bank[4], s_nc, t_idr)
            PE.quiet(mm(PS[4][:, 0:T], q[:, 144:272], k, True, False))
            PE.quiet(mm(PS[4][:, 0:T], e_r, NCH[:, :], False, False))
            k4 = PE.do(mm(PS[4][:, 0:T], e_r, NCL[:, :], False, True))
            PE.wait(bank[5])
            PE.quiet(mm(PS[5][:, 0:144], q[:, 16:144], k[:, 0:144], True, False))
            PE.quiet(mm(PS[5][:, 0:144], e_r, NCH[:, 0:144], False, False))
            k5 = PE.do(mm(PS[5][:, 0:144], e_r, NCL[:, 0:144], False, True))
            s2 = DV.do(stt(sm.SS[i][:, 0:272], PS[4][:, 0:T], CTT[:, 2, h:h + 1], cm[:], ALU.add, ALU.add),
                       k4, sm.s_free[i], fence, (s_c, 32))
            s1 = DV.do(stt(sm.SS[i][:, 272:416], PS[5][:, 0:144], CTT[:, 1, h:h + 1], cm[:, 128:272],
                           ALU.add, ALU.add), k5)
            bank[4], bank[5] = s2, s1
            PE.wait(bank[6])
            for t, (k0, k1) in enumerate(QT):
                kv = PE.do(ptr(PS[6][0:k1 - k0, 128 * t:128 * t + 128], v[:, k0:k1], 128))
            vf = heads.get(("vm", h - 2))
            a = AC.do(copy_act(VM[i][0:16, 0, :], PS[6][0:16, 0:128]), kv, vf, vm_init)
            b = AC.do(copy_act(VM[i][:, 1:3, :], PS[6][:, 128:384].rearrange("p (t c) -> p t c", t=2)), kv, vf)
            bank[6] = b
            heads[("v", h)] = [a, b]
            if m == 1:
                qkv_free[p] = [kv]
            heads[("s", h)] = [None, s1, s2]

        def step_re(h):
            sm.reduce_exp(h % 2, heads[("s", h)])

        def step_b(h):
            heads[("pt", h)] = sm.transposes(h % 2)

        def step_c(h):
            i = h % 2
            PE.wait(heads[("pt", h)], heads[("v", h)], bank[7])
            PE.quiet(mm(PS[7][:, 16:T], VM[i][:, 0, :], sm.PT0[0][:, 16:T], True, False))
            PE.quiet(mm(PS[7][:, 16:T], VM[i][:, 1, :], sm.PT1[0][:], False, False))
            t = PE.do(mm(PS[7][:, 144:T], VM[i][:, 2, :], sm.PT2[0][:], False, True))
            sm.pt_free = t
            heads[("vm", h)] = t
            s = split(PS[7][:, 16:T], OH[:, h, 16:T], OL[:, h, 16:T], t, fence)
            bank[7] = s
            ores[h] = (OH[:, h, :], OL[:, h, :], s)

        def take(dst, p, scale, key, n0):
            def evac(ps, tk):
                t = [AC.do(copy_act(dst[p][:, m, n0:T], ps[m], scale), tk[m], qkv_free[p]) for m in range(2)]
                heads[key] = heads.get(key, []) + t
                return t
            return evac

        rate[0] = 5
        for j in range(4):
            p = j % 2
            drain()
            gemm(A["attn_w_q"][0], KD, 256 * j, 2, xs, NMETA, T, take(QF, p, 1.0 / math.sqrt(128), j, NMETA))
            gemm(A["kv_w"], KD, 256 * j, 2, kxs, 0, T, take(KF_, p, 1.0, j, 0))
            gemm(A["kv_w"], KD, 1024 + 256 * j, 2, kxs, 0, T, take(VF, p, 1.0, j, 0))
            for h in (2 * j, 2 * j + 1):
                side += [lambda h=h: step_a(h), lambda h=h: h and step_b(h - 1), lambda h=h: step_re(h),
                         lambda h=h: h and step_c(h - 1), lambda h=h: sm.normalise(h % 2)]
        drain()
        step_b(7)
        step_c(7)
        rate[0] = 2
        for j in range(4):
            gemm(A["attn_w_o"][0], KD, 256 * j, 2, ores, NMETA, T, residual(j, NMETA))
    xs = layer_norm(4, XH, XL, NMETA)
    fg.close()
    ffn(A["ffn2_wg"][1], A["ffn2_wu"][1], A["ffn2_wd"][1], xs, NMETA)
    layer_norm(5, XH, XL, NMETA)
    fence = now()
    b1.close()

    b2 = ExitStack()
    SQ2 = sb(b2, [128, 4, T])
    UT = sb(b2, [128, 4, T])

    def rms_norm(key, n0, fence, emit):
        n = T - n0
        var_t, free = None, [fence, fence]
        for j in range(4):
            q = slice(2 * (j % 2), 2 * (j % 2) + 2)
            a = AC.do(fn_act(SQ2[:, q, 0:n], H[:, 2 * j:2 * j + 2, n0:T], ACT.Square),
                      h_t[2 * j], h_t[2 * j + 1], free[j % 2])
            for k in (2 * j, 2 * j + 1):
                f = mm(PS[6][:, 0:n], mean1[:], SQ2[:, k % 4, 0:n], k == 0, k == KD - 1)
                var_t = PE.do(f, a, bank[6] if k == 0 else None)
            free[j % 2] = var_t
        a, r = rstd(PS[6][:, 0:n], var_t, 1, n)
        bank[6] = a
        u_free = [fence, fence]
        for j in range(4):
            q = slice(2 * (j % 2), 2 * (j % 2) + 2)
            rb = RS[:, 0:n].unsqueeze(1).to_broadcast([128, 2, n])
            d = DV.do(tt(UT[:, q, 0:n], H[:, 2 * j:2 * j + 2, n0:T], rb, ALU.mult), r, u_free[j % 2],
                      h_t[2 * j], h_t[2 * j + 1])
            u_free[j % 2] = [emit(k, UT[:, k % 4, 0:n], d, pc(key, k)) for k in (2 * j, 2 * j + 1)]

    def normed(key, n0, fence):
        res = []

        def emit(k, u, d, w):
            hi, lo = XH[:, k, n0:T], XL[:, k, n0:T]
            a1 = AC.do(fn_act(hi, u, ACT.Copy, scale=w), d, p_t)
            l = DV.do(stt(lo, u, w, hi.bitcast(F32), ALU.mult, ALU.subtract), a1)
            res.append((XH[:, k, :], XL[:, k, :], [a1, l]))
            return l
        rms_norm(key, n0, fence, emit)
        return res

    us = normed("norm_mix_w_2", 0, fence)
    W_IN = A["w_in_2"][0]
    Z0, X_0, DT0, Q0, K0, GS0, GA0 = 0, 2048, 5120, 5152, 6176, 6432, 7456

    ma = ExitStack()
    GA = sb(ma, [128, KD, NV])
    ZS = sb(ma, [128, 16, NV])
    fence0 = now()
    with ExitStack() as st:
        fence = now()
        AH, AL = sb(st, [128, KD, NV], F32R), sb(st, [128, KD, NV], F32R)
        SNK = sb(st, [128, 16])
        B2 = sb(st, [128, 16, 272])
        B1 = sb(st, [128, 16, 16])
        B0 = sb(st, [16, 16, 16])
        QR = [sb(st, [128, T]) for _ in range(8)]
        KZ = [[sb(st, [128, T]) for _ in range(2)] for _ in range(2)]
        VV = sb(st, [128, T])
        VM = sb(st, [128, 3, 128])
        sm = Softmax(st, fence, (2, 1, 0))
        sk = A["attn_sinks_2"]
        GP.dma(lambda e: e.dma_start(SNK[:], bass.AP(tensor=sk.tensor, offset=sk.offset, ap=[[0, 128], [1, 16]])),
               s_b, fence)
        PT_ = 16 * WS

        def shifted(off, nq, n):
            return bass.AP(tensor=sv.tensor, offset=sv.offset + off, ap=[[PT_ - 1, nq], [WS, 16], [1, n]])
        GP.dma(lambda e: e.dma_start(B2[:, :, 16:272], shifted(127, 128, 256)), s_b, (s_b, 64))
        GP.dma(lambda e: e.dma_start(B2[:, :, 0:16], shifted(STRIP + 271 - 144, 128, 16)), s_b)
        GP.dma(lambda e: e.dma_start(B1[:], shifted(STRIP + 271 - 16, 128, 16)), s_b)
        GP.dma(lambda e: e.dma_start(B0[:], shifted(STRIP + 271, 16, 16)), s_b)
        bias_in = (s_b, 64 + 80)
        kz_init = zero_pad([KZ[0][0], KZ[0][1], KZ[1][0], KZ[1][1], VM], fence)
        q_t = [None] * 8
        kv_t = []
        ares = [None] * 8

        def evac_q(j):
            def evac(ps, tk):
                t = [AC.do(copy_act(QR[2 * j + m][:], ps[m], 0.125), tk[m], fence) for m in range(2)]
                q_t[2 * j], q_t[2 * j + 1] = t
                return t
            return evac

        def evac_kv(ps, tk):
            for g in range(2):
                for par in range(2):
                    o = KZ[par][g][64 * par:64 * par + 64, :]
                    kv_t.append(AC.do(copy_act(o, ps[0][64 * g:64 * g + 64, :]), tk[0], kz_init))
            v = DV.do(lambda e: e.tensor_copy(VV[:], ps[1]), tk[1], fence)

            def vt():
                PE.wait(v, bank[6])
                for t, (k0, k1) in enumerate(QT):
                    k = PE.do(ptr(PS[6][0:k1 - k0, 128 * t:128 * t + 128], VV[:, k0:k1], 128))
                a = AC.do(copy_act(VM[0:16, 0, :], PS[6][0:16, 0:128]), k, kz_init)
                b = AC.do(copy_act(VM[:, 1:3, :], PS[6][:, 128:384].rearrange("p (t c) -> p t c", t=2)), k)
                bank[6] = b
                kv_t.extend([a, b])
            side.append(vt)
            return [kv_t[3], v]

        pts = {}

        def swa_a(h):
            c, par, g, i = h // 2, h % 2, h // 8, h % 2
            q, kz = QR[c], KZ[par][g]
            PE.wait(q_t[c], kv_t, bank[4])
            k4 = PE.do(mm(PS[4][:, 0:T], q[:, 144:272], kz[:]))
            PE.wait(bank[5])
            PE.quiet(mm(PS[5][:, 0:144], q[:, 16:144], kz[:, 0:144]))
            k5 = PE.do(mm(PS[5][0:16, 144:160], q[:, 0:16], kz[:, 0:16]))
            SS = sm.SS[i]
            s2 = DV.do(tt(SS[:, 0:272], PS[4][:, 0:T], B2[:, h, :], ALU.add), k4, bias_in, sm.s_free[i], fence)
            DV.do(tt(SS[:, 272:288], PS[5][:, 0:16], B1[:, h, :], ALU.add), k5)
            s1 = DV.do(tt(SS[:, 288:416], PS[5][:, 16:144], B2[:, h, 144:272], ALU.add))
            s0 = DV.do(tt(SS[0:16, 416:432], PS[5][0:16, 144:160], B0[:, h, :], ALU.add))
            bank[4], bank[5] = s2, s0
            pts[("s", h)] = [s0, s1, s2]

        def swa_re(h):
            sm.reduce_exp(h % 2, pts[("s", h)], SNK[:, h:h + 1])

        def swa_b(h):
            pts[h] = sm.transposes(h % 2)

        def swa_c(h):
            c, par, g, i = h // 2, h % 2, h // 8, h % 2
            PE.wait(pts[h], kv_t, bank[7])
            oo = PS[7][64 * par:64 * par + 64, :]
            gs = slice(64 * g, 64 * g + 64)
            PE.quiet(mm(oo[:, 0:T], VM[:, 0, gs], sm.PT0[0][:], True, False))
            PE.quiet(mm(oo[:, 16:T], VM[:, 1, gs], sm.PT1[0][:], False, False))
            t = PE.do(mm(oo[:, 144:T], VM[:, 2, gs], sm.PT2[0][:], False, True))
            sm.pt_free = t
            pp = slice(64 * par, 64 * par + 64)
            s = split(oo[:, TS:T], AH[pp, c, :], AL[pp, c, :], t, fence)
            bank[7] = s
            if par == 0:
                ares[c] = (AH[:, c, :], AL[:, c, :], s)
            else:
                ares[c] = (ares[c][0], ares[c][1], ares[c][2] + s)

        def keep(dst, j, *after):
            def evac(ps, tk):
                return [AC.do(copy_act(dst[:, 2 * j + m, :], ps[m]), tk[m], *after) for m in range(2)]
            return evac

        gemm(W_IN, KD, K0, 2, us, 0, T, evac_kv)
        for j in range(4):
            gemm(W_IN, KD, Q0 + 256 * j, 2, us, 0, T, evac_q(j))
        drain()
        for h in range(17):
            if h < 16:
                side.append(lambda h=h: swa_a(h))
            if h:
                side.append(lambda h=h: swa_b(h - 1))
            if h < 16:
                side.append(lambda h=h: swa_re(h))
            if h:
                side.append(lambda h=h: swa_c(h - 1))
            if h < 16:
                side.append(lambda h=h: sm.normalise(h % 2))
        rate[0] = 7
        for j in range(8):
            gemm(W_IN, KD, Z0 + 256 * j, 2, us, TS, T, keep(ZS, j, fence0))
        for j in range(4):
            gemm(W_IN, KD, GA0 + 256 * j, 2, us, TS, T, keep(GA, j, fence0))
        drain()
        rate[0] = 2
        last = (AC.sem, AC.n)
        g_t = [AC.do(fn_act(GA[:, k, :], GA[:, k, :], ACT.Sigmoid, bias=pc("gate_b_2", 8 + k)), last, p_t)
               for k in range(KD)]
        ga_t = [None] * KD
        z_t = [None] * 16

        def silu_z(k):
            z_t[k] = AC.do(fn_act(ZS[:, k, :], ZS[:, k, :], ACT.Silu), last)
        side += [lambda k=k: silu_z(k) for k in range(16)]
        rate[0] = 6

        def evac_ya(j):
            def evac(ps, tk):
                t = [DV.do(tt(GA[:, 2 * j + m, :], GA[:, 2 * j + m, :], ps[m], ALU.mult), tk[m], g_t[2 * j + m])
                     for m in range(2)]
                ga_t[2 * j:2 * j + 2] = t
                return t
            return evac
        for j in range(4):
            gemm(A["w_attn_branch_2"][0], KD, 256 * j, 2, ares, 0, NV, evac_ya(j))
        drain()

    Y = None
    ys = ExitStack()
    fence = now()
    YB = sb(ys, [128, 16, NV])
    y_t = [None] * 16
    with ExitStack() as st:
        BC = sb(st, [128, 8, T])
        CBM = sb(st, [128, 4, 432])
        ZD = sb(st, [32, T])
        LD = sb(st, [32, T])
        DTB, AL_, DC, DC2 = sb(st, [32, 1]), sb(st, [32, 1]), sb(st, [128, 16]), sb(st, [128, 32])
        CSB = [sb(st, [128, 256 + T]) for _ in range(2)]
        CSH, CSL = sb(st, [128, T], F32R), sb(st, [128, T], F32R)
        DTT, NCT = sb(st, [128, 3, 32]), sb(st, [128, 3, 32])
        CY = [sb(st, [128, 2, T]) for _ in range(2)]
        XDT = [sb(st, [128, 3, 128]) for _ in range(2)]
        EX = [sb(st, [128, 432]) for _ in range(4)]
        s_d = sem("s_d")
        GP.dma(lambda e: e.dma_start(DTB[:], A["ssd_dt_bias_2"].rearrange("l p -> p l")), s_d, fence)
        GP.dma(lambda e: e.dma_start(AL_[:], A["ssd_a_log_2"].rearrange("l p -> p l")), s_d)
        dd = A["ssd_d_2"]
        GP.dma(lambda e: e.dma_start(
            DC2[:], bass.AP(tensor=dd.tensor, offset=dd.offset, ap=[[0, 128], [1, 32]])), s_d)
        d_in = (s_d, 48)
        dc_t = [AC.do(copy_act(DC[64 * a:64 * a + 64, :],
                               DC2[64 * a:64 * a + 64, :].rearrange("p (c a) -> p c a", a=2)[:, :, a]), d_in, fence)
                for a in range(2)]
        cs_zero = zero_pad(CSB, fence)
        dt = {}
        w = {}

        def neg_a():
            a = AC.do(fn_act(AL_[:], AL_[:], ACT.Exp), d_in)
            w["a"] = DV.do(ts(AL_[:], AL_[:], -1.0, None, ALU.mult), a)

        def dt_done():
            w["dt"] = w["t"] = DV.do(stt(ZD[:], ZD[:], 0.0, LD[:], ALU.max, ALU.add), w["t"])

        def log_decay():
            w["t"] = DV.do(ts(CSB[0][0:32, 256:256 + T], ZD[:], AL_[:, 0:1], None, ALU.mult),
                           w["t"], w["a"], cs_zero)
        C = CSB[1][:, 256:256 + T]

        def decay_split():
            w["s"] = split(C, CSH[:], CSL[:], w["t"])

        def decay_T():
            PE.wait(bank[6], w["dt"], w["t"])
            for i, (t0, t1) in enumerate(ST):
                PE.quiet(ptr(PS[6][0:t1 - t0, 32 * i:32 * i + 32], ZD[:, t0:t1], 32))
                k = PE.do(ptr(PS[6][0:t1 - t0, 96 + 32 * i:128 + 32 * i], C[0:32, t0:t1], 32))
            r = []
            for o, dst, sc in ((0, DTT, 1.0), (96, NCT, -1.0)):
                r.append(AC.do(copy_act(dst[:, 0:2, :], PS[6][:, o:o + 64].rearrange("p (a c) -> p a c", a=2),
                                        sc), k, fence))
                r.append(AC.do(copy_act(dst[0:16, 2, :], PS[6][0:16, o + 64:o + 96], sc), k))
            bank[6] = r[-1]
            dt["t"] = r + w["s"]

        def evac_dt(ps, tk):
            z = w["t"] = AC.do(fn_act(ZD[:], ps[0][0:32, :], ACT.Identity, bias=DTB[:, 0:1]), tk[0], d_in, fence)
            side.extend(softplus_steps(ZD[:], 32, LD[:], w) + [dt_done, neg_a, log_decay]
                        + cumsum_steps(CSB, 32, w) + [decay_split, decay_T])
            return [z]

        def conv(ps, tk, c, dst, free):
            p = [pc("ssd_conv_w_2", 24 * 3 + c + m) for m in range(2)]
            y = [AC.do(fn_act(dst[m], ps[m], ACT.Copy, scale=p[m]), tk[m], p_t, free) for m in range(2)]
            for o in (1, 2, 3):
                y = [DV.do(stt(dst[m][:, o:T], ps[m][:, 0:T - o], pc("ssd_conv_w_2", 24 * (3 - o) + c + m),
                               dst[m][:, o:T], ALU.mult, ALU.add), y[m]) for m in range(2)]
            z = [AC.do(fn_act(dst[m], dst[m], ACT.Silu, bias=pc("ssd_conv_b_2", c + m)), y[m]) for m in range(2)]
            return y, z

        gemm(W_IN, KD, DT0, 1, us, 0, T, evac_dt)
        rate[0] = 6
        bc_t = [None] * 8
        for j in range(4):
            def evac_bc(ps, tk):
                y, z = conv(ps, tk, 16 + 2 * j, [BC[:, 2 * j + m, :] for m in range(2)], fence)
                bc_t[2 * j:2 * j + 2] = z
                return y
            gemm(W_IN, KD, X_0 + 2048 + 256 * j, 2, us, 0, T, evac_bc)
        cb_t = [None] * 4

        def cb(g):
            b = 4 + g % 2
            B, C = BC[:, g, :], BC[:, 4 + g, :]
            PE.wait(bc_t[g], bc_t[4 + g], bank[b], bank[7])
            PE.quiet(mm(PS[b][:, 0:272], B[:, 0:128], C[:, :]))
            k1 = PE.do(mm(PS[b][:, 272:416], B[:, 128:256], C[:, 128:272]))
            k2 = PE.do(mm(PS[7][0:16, 0:16], B[:, 256:272], C[:, 256:272]))
            d = DV.do(tt(CBM[:, g, 0:416], PS[b][:, 0:416], tri[:, 0:416], ALU.mult), k1, fence, (s_c, 32))
            d2 = DV.do(tt(CBM[0:16, g, 416:432], PS[7][0:16, 0:16], tri[0:16, 416:432], ALU.mult), k2)
            bank[b], bank[7] = d, d2
            cb_t[g] = [d, d2]
        for g in range(4):
            side.append(lambda g=g: cb(g))
        xdt_free, xs_free = [fence, fence], [fence, fence]
        ex_free, m_free = [None] * 4, [None] * 4
        xs_t, m_t, xd_t, e_t = {}, {}, {}, {}

        def ssd_x(c):
            p = c % 2
            x = CY[(c // 2) % 2][:, c % 2, :]
            PE.wait(bank[6], xs_t[c])
            for i, (t0, t1) in enumerate(ST):
                k = PE.do(ptr(PS[6][0:t1 - t0, 128 * i:128 * i + 128], x[:, t0:t1], 128))
            o = XDT[p][:, 0:2, :].rearrange("p t (h d) -> p t h d", h=2)
            src = PS[6][:, 0:256].rearrange("p (t h d) -> p t h d", t=2, h=2)
            d = DV.do(tt(o, src, DTT[:, 0:2, 2 * c:2 * c + 2].unsqueeze(3).to_broadcast([128, 2, 2, 64]), ALU.mult),
                      k, dt["t"], xdt_free[p])
            o2 = XDT[p][0:16, 2, :].rearrange("p (h d) -> p h d", h=2)
            s2 = PS[6][0:16, 256:384].rearrange("p (h d) -> p h d", h=2)
            d2 = DV.do(tt(o2, s2, DTT[0:16, 2, 2 * c:2 * c + 2].unsqueeze(2).to_broadcast([16, 2, 64]), ALU.mult), k)
            bank[6] = d2
            xd_t[c] = [d, d2]

        def ssd_e(h):
            b, i = 4 + h % 2, h % 4
            e_r = identR[:, h:h + 1].to_broadcast([128, 128])
            PE.wait(bank[b], dt["t"], t_idr)
            PE.quiet(mm(PS[b][:, 0:T], e_r, CSH[:, :], True, False))
            k = PE.do(mm(PS[b][:, 0:T], e_r, CSL[:, :], False, True))
            E = EX[i]
            DV.do(ts(E[:, 0:272], PS[b][:, 0:T], NCT[:, 0, h:h + 1], 0.0, ALU.add, ALU.min),
                  k, dt["t"], m_free[i], fence)
            c1 = DV.do(ts(E[:, 272:416], PS[b][:, 128:T], NCT[:, 1, h:h + 1], 0.0, ALU.add, ALU.min))
            c2 = DV.do(ts(E[0:16, 416:432], PS[b][0:16, 256:T], NCT[0:16, 2, h:h + 1], 0.0, ALU.add, ALU.min))
            bank[b] = c2
            e_t[h] = [AC.do(fn_act(E[:, 0:416], E[:, 0:416], ACT.Exp), c1),
                      AC.do(fn_act(E[0:16, 416:432], E[0:16, 416:432], ACT.Exp), c2)]

        def ssd_m(h):
            E, g = EX[h % 4], h // 8
            m_t[h] = [GP.do(tt(E[:, 0:416], E[:, 0:416], CBM[:, g, 0:416], ALU.mult), e_t[h], cb_t[g]),
                      GP.do(tt(E[0:16, 416:432], E[0:16, 416:432], CBM[0:16, g, 416:432], ALU.mult))]

        def ssd_y(c):
            p = c % 2
            PE.wait(bank[7], xd_t[c])
            for par in range(2):
                h = 2 * c + par
                M = EX[h % 4]
                o = PS[7][64 * par:64 * par + 64, :]
                hs = slice(64 * par, 64 * par + 64)
                PE.wait(m_t[h])
                PE.quiet(mm(o[:, 0:T], XDT[p][:, 0, hs], M[:, 0:272], True, False))
                PE.quiet(mm(o[:, 128:T], XDT[p][:, 1, hs], M[:, 272:416], False, False))
                k = PE.do(mm(o[:, 256:T], XDT[p][0:16, 2, hs], M[0:16, 416:432], False, True))
                m_free[h % 4] = k
            xdt_free[p] = k
            x = CY[(c // 2) % 2][:, c % 2, TS:T]
            d = DV.do(stt(YB[:, c, :], x, DC[:, c:c + 1], PS[7][:, TS:T], ALU.mult, ALU.add), k, dc_t, fence)
            bank[7] = d
            xs_free[(c // 2) % 2] = [d]
            y_t[c] = GP.do(tt(YB[:, c, :], YB[:, c, :], ZS[:, c, :], ALU.mult), d, z_t[c])

        drain()
        rate[0] = 8
        tail = []
        for j in range(8):
            def evac_xs(ps, tk):
                s = j % 2
                y, z = conv(ps, tk, 2 * j, [CY[s][:, m, :] for m in range(2)], xs_free[s])
                xs_t[2 * j], xs_t[2 * j + 1] = z
                return y
            gemm(W_IN, KD, X_0 + 256 * j, 2, us, 0, T, evac_xs)
            drain()
            for c in (2 * j, 2 * j + 1):
                side.append(lambda c=c: ssd_x(c))
                side.append(lambda c=c: ssd_e(2 * c))
                if c:
                    side.append(lambda c=c: ssd_y(c - 1))
                side.append(lambda c=c: ssd_e(2 * c + 1))
                side.append(lambda c=c: (ssd_m(2 * c), ssd_m(2 * c + 1)))
        side.append(lambda: ssd_y(15))
        drain()
        rate[0] = 2
        fence = now()
    fin = ExitStack()
    YH, YL = sb(fin, [128, 16, NV], F32R), sb(fin, [128, 16, NV], F32R)
    SY = sb(fin, [128, 4, NV])
    GS = sb(fin, [128, KD, NV])
    gs_t = [None] * KD
    yres = []

    gn = {}

    def gn_sum(g):
        s = slice(4 * g, 4 * g + 4)
        a = AC.do(fn_act(SY[:], YB[:, s, :], ACT.Square), y_t[4 * g:4 * g + 4], fence, gn.get("sy"))
        PE.wait(a, bank[6])
        for k in range(4):
            t = PE.do(mm(PS[6][:, 0:NV], mean5[:], SY[:, k, :], k == 0, k == 3))
        gn["sy"] = t
        gn[g] = t

    def gn_rstd(g):
        s = slice(4 * g, 4 * g + 4)
        a, r = rstd(PS[6][:, 0:NV], gn[g], 1, NV)
        bank[6] = a
        rb = RS[:, 0:NV].unsqueeze(1).to_broadcast([128, 4, NV])
        gn[g] = DV.do(tt(YB[:, s, :], YB[:, s, :], rb, ALU.mult), r)

    def gn_out(k):
        w = pc("ssd_norm_w_2", k)
        a = AC.do(fn_act(YH[:, k, :], YB[:, k, :], ACT.Copy, scale=w), gn[k // 4])
        l = DV.do(stt(YL[:, k, :], YB[:, k, :], w, YH[:, k, :].bitcast(F32), ALU.mult, ALU.subtract), a)
        yres.append((YH[:, k, :], YL[:, k, :], [a, l]))
    for g in range(4):
        side.append(lambda g=g: gn_sum(g))
        side.append(lambda g=g: gn_rstd(g))
        side += [lambda k=k: gn_out(k) for k in range(4 * g, 4 * g + 4)]
    rate[0] = 8
    last = now()
    warm = [AC.do(fn_act(cc[:, 3:4], cc[:, 2:3], ACT.Ln), m_c)]
    for j in range(4):
        def evac_gs(ps, tk):
            t = [AC.do(copy_act(GS[:, 2 * j + m, :], ps[m]), tk[m], fence) for m in range(2)]
            gs_t[2 * j:2 * j + 2] = t
            return t
        gemm(W_IN, KD, GS0 + 256 * j, 2, us, TS, T, evac_gs)
    drain()
    rate[0] = 2
    for k in range(KD):
        gs_t[k] = AC.do(fn_act(GS[:, k, :], GS[:, k, :], ACT.Sigmoid, bias=pc("gate_b_2", k)), gs_t[k])
    x_free = now()
    mres = []
    for j in range(4):
        def evac_ys(ps, tk):
            t = [DV.do(tt(GS[:, 2 * j + m, :], GS[:, 2 * j + m, :], ps[m], ALU.mult), tk[m], gs_t[2 * j + m])
                 for m in range(2)]
            for m in range(2):
                k = 2 * j + m
                d = DV.do(tt(GS[:, k, :], GS[:, k, :], GA[:, k, :], ALU.add), t[m], ga_t[k])
                s = split(GS[:, k, :], XH[:, k, TS:T], XL[:, k, TS:T], d, x_free)
                mres.append((XH[:, k, :], XL[:, k, :], s))
            return t
        gemm(A["w_ssd_branch_2"][0], 16, 256 * j, 2, yres, 0, NV, evac_ys)

    def add_h(j, n0):
        def evac(ps, tk):
            t = [DV.do(tt(H[:, 2 * j + m, n0:T], H[:, 2 * j + m, n0:T], ps[m], ALU.add), tk[m], h_t[2 * j + m])
                 for m in range(2)]
            h_t[2 * j:2 * j + 2] = t
            return t
        return evac
    for j in range(4):
        gemm(A["w_out_2"][0], KD, 256 * j, 2, mres, TS, T, add_h(j, TS))
    fence = now()
    fin.close()
    ys.close()
    ma.close()

    us = normed("norm_ffn_w_2", TS, fence)
    NO = T - NMETA
    with ExitStack() as st:
        HH, HL = sb(st, [128, KF, NO], F32R), sb(st, [128, KF, NO], F32R)
        UP = [sb(st, [128, 2, NO]) for _ in range(2)]
        GT = [sb(st, [128, 2, NO]) for _ in range(2)]
        free = [fence, fence]
        hid, up_t = [], [None]
        ring[0] = (0, 2, 4)

        def fw(tap, c):
            return pc("fw01", 44 * tap + c) if tap < 2 else pc("fw2", c)

        def conv3(ps, tk, c, dst, free):
            y = [AC.do(fn_act(dst[:, m, :], ps[m][:, 2:2 + NO], ACT.Identity, scale=fw(2, c + m),
                              bias=pc("ffn_conv_b_2", c + m)), tk[m], free) for m in range(2)]
            for o in (1, 0):
                y = [DV.do(stt(dst[:, m, :], ps[m][:, o:o + NO], fw(o, c + m), dst[:, m, :], ALU.mult, ALU.add),
                           y[m]) for m in range(2)]
            return y
        for j in range(11):
            s = j % 2

            def evac_g(ps, tk):
                y = conv3(ps, tk, 22 + 2 * j, GT[s], free[s])
                up_t[0] = [AC.do(fn_act(GT[s][:, m, :], GT[s][:, m, :], ACT.Silu), y[m]) for m in range(2)]
                return y

            def evac_u(ps, tk):
                y = conv3(ps, tk, 2 * j, UP[s], free[s])
                d = [DV.do(tt(UP[s][:, m, :], UP[s][:, m, :], GT[s][:, m, :], ALU.mult), y[m], up_t[0][m])
                     for m in range(2)]
                hs = [split(UP[s][:, m, :], HH[:, 2 * j + m, :], HL[:, 2 * j + m, :], d[m], fence) for m in range(2)]
                free[s] = hs[0] + hs[1]
                hid.extend((HH[:, 2 * j + m, :], HL[:, 2 * j + m, :], hs[m]) for m in range(2))
                return y
            gemm(A["w_ffn_in_2"][0], KD, FF + 256 * j, 2, us, TS, T, evac_g)
            gemm(A["w_ffn_in_2"][0], KD, 256 * j, 2, us, TS, T, evac_u)
        for j in range(4):
            gemm(A["w_ffn_out_2"][0], KF, 256 * j, 2, hid, 0, NO, add_h(j, NMETA))
        fence = now()

    OT = sb(b2, [128, 2, D])
    FN = sb(b2, [128, 4, NO])
    s_out = sem("s_out")
    o_t = []
    fn_free = [fence, fence]

    def emit(k, u, d, w):
        i = k % 4
        a = AC.do(fn_act(FN[:, i, :], u, ACT.Copy, scale=w), d, fn_free[(k // 2) % 2])
        b = 4 + k % 2
        PE.wait(a, bank[b])
        PE.quiet(ptr(PS[b][:, 0:128], FN[:, i, 0:128], 128))
        t = PE.do(ptr(PS[b][:, 128:256], FN[:, i, 128:256], 128))
        fn_free[(k // 2) % 2] = [t]
        o = DV.do(lambda e: e.tensor_copy(OT[:, :, k * 128:k * 128 + 128],
                                          PS[b][:, 0:256].rearrange("p (t c) -> p t c", t=2)), t, fence)
        bank[b] = o
        o_t.append(o)
        return a
    rms_norm("norm_final_w_2", NMETA, fence, emit)
    for half in range(2):
        SP.dma(lambda e, half=half: e.dma_start(
            out[0].rearrange("(t p) c -> p t c", p=128)[:, :, 512 * half:512 * half + 512],
            OT[:, :, 512 * half:512 * half + 512]), s_out, o_t[4 * half:4 * half + 4])
    SP.wait((s_out, 32))
    b2.close()

    block = ctx.enter_context(nc.Block())

    @block.sync
    def _(e):
        SP.run(e)

    @block.gpsimd
    def _(e):
        GP.run(e)

    @block.scalar
    def _(e):
        AC.run(e)

    @block.vector
    def _(e):
        DV.run(e)

    @block.tensor
    def _(e):
        PE.run(e)


def kernel(**inputs):
    import concourse.bacc as bacc
    from concourse.bass_utils import run_bass_kernel_spmd

    nc = bacc.Bacc("TRN2", target_bir_lowering=False, num_devices=1)
    arrays = {n: np.ascontiguousarray(a) for n, a in inputs.items()}
    arrays.update(constants())
    arrays = {f"in_{n}": a for n, a in arrays.items()}
    A = {n[3:]: nc.dram_tensor(n, a.shape, mybir.dt.from_np(a.dtype), kind="ExternalInput").ap()
         for n, a in arrays.items()}
    out = nc.dram_tensor("out_y", (1, 256, 1024), F32, kind="ExternalOutput").ap()
    scratch = nc.dram_tensor("strips", (128, 16, STRIP + MSTRIP), F32, kind="Internal").ap()
    program(nc, A, out, scratch)
    r = run_bass_kernel_spmd(nc, [arrays], core_ids=[0])
    return r.results[0]["out_y"]
```

```python
import math
from contextlib import ExitStack

import numpy as np
import concourse.bass as bass
from concourse import mybir
from concourse.alu_op_type import AluOpType as ALU

F32 = mybir.dt.float32
F32R = mybir.dt.float32r
ACT = mybir.ActivationFunctionType
AX = mybir.AxisListType

T = 272
NMETA = 16
D = 1024
KD = 8
FF = 2816
KF = 22
ALPHA = 4 ** 0.25
QT = ((0, 16), (16, 144), (144, 272))
ST = ((0, 128), (128, 256), (256, 272))
TS = 14
NV = T - TS
NEG = -1e30
STRIP = 384
MSTRIP = 288


def constants():
    ident = np.eye(128, dtype=np.float32)
    causal = np.where(np.arange(128)[None, :] <= np.arange(128)[:, None], 0.0, NEG).astype(np.float32)
    cm = np.concatenate([np.zeros((128, 144), np.float32), causal], axis=1)
    tri = (np.arange(128)[None, :] >= np.arange(128)[:, None]).astype(np.float32)
    one = np.ones((128, 144), np.float32)
    t432 = np.concatenate([tri, one, tri, one[:, :16], tri[:, :16]], axis=1)

    def bucket(dist):
        d = np.maximum(dist, 0)
        big = 16 + (np.log(np.maximum(d, 16).astype(np.float32) / np.float32(16))
                    / np.float32(math.log(128 / 16)) * np.float32(16)).astype(np.int32)
        return np.where(d < 16, d, np.minimum(big, 31))

    db, dm = 255 - np.arange(STRIP), 271 - np.arange(MSTRIP)
    both = np.concatenate([db, dm])
    hot = (bucket(both)[None, :] == np.arange(32)[:, None]).astype(np.float32)
    ok = np.concatenate([(db >= 0) & (db < 128), dm >= 0])
    smask = np.broadcast_to(np.where(ok, 0.0, NEG).astype(np.float32), (16, both.size))
    return {"c_ident": ident, "c_cm": cm, "c_tri": t432, "c_hot": hot,
            "c_smask": np.ascontiguousarray(smask)}


PENDING = "freed by a side step that is still to come"


class Queue:

    def __init__(self, sem):
        self.items, self.sem, self.n = [], sem, 0

    def wait(self, *tickets):
        for t in tickets:
            if t is None:
                continue
            if isinstance(t, list):
                self.wait(*t)
            else:
                self.items.append(("wait", t[0], t[1]))

    def quiet(self, fn, *after):
        self.wait(*after)
        self.items.append(("run", fn, None, 0))

    def do(self, fn, *after):
        self.wait(*after)
        self.n += 1
        self.items.append(("run", fn, self.sem, 1))
        return (self.sem, self.n)

    def dma(self, fn, sem, *after):
        self.wait(*after)
        self.items.append(("run", fn, sem, 16))

    def place(self):
        inner = Queue(None)
        self.items.append(("place", inner))
        return inner

    def run(self, eng, seen=None):
        seen = {} if seen is None else seen
        for it in self.items:
            if it[0] == "wait":
                if seen.get(id(it[1]), 0) < it[2]:
                    seen[id(it[1])] = it[2]
                    eng.wait_ge(it[1], it[2])
            elif it[0] == "place":
                it[1].run(eng, seen)
            else:
                ins = it[1](eng)
                if it[2] is not None:
                    ins.then_inc(it[2], it[3])


def program(nc, A, out, scratch):
    ctx = ExitStack()
    with ctx:
        build(nc, A, out, scratch, ctx)


def build(nc, A, out, scratch, ctx):
    uid = [0]

    def sb(stack, shape, dt=F32):
        uid[0] += 1
        return stack.enter_context(nc.sbuf_tensor(f"t{uid[0]}", shape, dt))

    def sem(name):
        return ctx.enter_context(nc.semaphore(name))

    PE, AC, DV, GP, SP = (Queue(sem(f"s_{n}")) for n in ("pe", "act", "dve", "pool", "sp"))

    NR, NH, LA = 4, 3, 2
    raw = [sb(ctx, [128, 2048]) for _ in range(NR)]
    wh = [sb(ctx, [128, 2048], F32R) for _ in range(NH)]
    wl = [sb(ctx, [128, 2048], F32R) for _ in range(NH)]
    H = sb(ctx, [128, KD, T])
    XH = sb(ctx, [128, KD, T], F32R)
    XL = sb(ctx, [128, KD, T], F32R)
    PV = sb(ctx, [128, 4, 128])
    ident = sb(ctx, [128, 128])
    identR = sb(ctx, [128, 128], F32R)
    mean1 = sb(ctx, [128, 128])
    mean5 = sb(ctx, [128, 128])
    cm = sb(ctx, [128, T])
    tri = sb(ctx, [128, 432])
    RS = sb(ctx, [128, T])
    LNV = sb(ctx, [128, T])
    cc = sb(ctx, [128, 4])
    PS = [ctx.enter_context(nc.psum_tensor(f"ps{i}", [128, 512], F32)) for i in range(8)]
    bank = [None] * 8

    s_c, s_x, s_p = sem("s_c"), sem("s_x"), sem("s_p")
    b1 = ExitStack()
    WF, FB, RB = sb(b1, [128, KD, 8]), sb(b1, [8, 1]), sb(b1, [32, 16])
    cstk = ExitStack()
    XC = sb(b1, [128, KD, T])
    prow = XC[:, 0:2, :].rearrange("p a c -> p (a c)")[:, 0:512].rearrange("p (a c) -> p a c", a=4)
    X0, X1, X2 = sb(cstk, [16, D]), sb(cstk, [128, D]), sb(cstk, [128, D])
    SP.dma(lambda e: e.dma_start(ident[:], A["c_ident"]), s_x)
    SP.dma(lambda e: e.dma_start(X0[:], A["meta"]), s_x)
    SP.dma(lambda e: e.dma_start(X1[:], A["x"][0, 0:128, :]), s_x)
    SP.dma(lambda e: e.dma_start(X2[:], A["x"][0, 128:256, :]), s_x)
    x_in = (s_x, 64)
    s_raw = [sem(f"s_raw{i}") for i in range(NR)]
    GP.wait((s_raw[0], 16))
    GP.dma(lambda e: e.dma_start(cm[:], A["c_cm"]), s_c)
    GP.dma(lambda e: e.dma_start(tri[:], A["c_tri"]), s_c)

    rows = [
        [("ln_gain", "l a (c p) -> (l a c) p"), ("ln_bias", "l a (c p) -> (l a c) p"),
         ("conv_w", "l k (c p) -> (l k c) p"), ("norm_mix_w_2", "l (c p) -> (l c) p")],
        [("ssd_conv_w_2", "l k (c p) -> (l k c) p"), ("ssd_conv_b_2", "l (c p) -> (l c) p"),
         ("norm_ffn_w_2", "l (c p) -> (l c) p")],
        [("ffn_conv_w_2", None), ("norm_final_w_2", "(c p) -> c p"),
         ("ssd_norm_w_2", "l (c p) -> (l c) p"), ("gate_b_2", "l a (c p) -> (l a c) p")],
        [("ffn_conv_w_2", None), ("ffn_conv_b_2", "l (c p) -> (l c) p")],
    ]
    col = {}
    nrow, n_p = [0] * 4, 0
    for t, parts in enumerate(rows):
        for name, how in parts:
            if how is None:
                v = A[name].rearrange("l k (c p) -> (l k c) p", p=128)
                v, key = (v[0:88], "fw01") if t == 2 else (v[88:132], "fw2")
            else:
                v, key = A[name].rearrange(how, p=128), name
            r0, n = nrow[t], v.shape[0]
            GP.dma(lambda e, t=t, r0=r0, n=n, v=v: e.dma_start(prow[r0:r0 + n, t, :], v), s_p)
            col[key] = (t, r0)
            nrow[t] += n
            n_p += 16

    def pc(key, i):
        t, r0 = col[key]
        return PV[:, t, r0 + i:r0 + i + 1]

    s_f, s_b = sem("s_f"), sem("s_b")
    GP.dma(lambda e: e.dma_start(WF[:], A["kv_w"][:, 2048:2056].rearrange("(k p) c -> p k c", p=128)), s_f)
    GP.dma(lambda e: e.dma_start(FB[:], A["f_bias"].rearrange("(p a) -> p a", a=1)), s_f)
    GP.dma(lambda e: e.dma_start(RB[:], A["rel_bias_2"]), s_f)
    m_c = DV.do(lambda e: e.memset(mean1[:], 1.0 / 1024))
    DV.do(lambda e: e.memset(mean5[:], 1.0 / 512))
    DV.do(lambda e: e.memset(cc[:, 0:1], 1e-5))
    DV.do(lambda e: e.memset(cc[:, 1:2], 1e-6))
    m_c = DV.do(lambda e: e.memset(cc[:, 2:3], 1.0))
    AC.quiet(lambda e: e.preload_act_table_set("silu_and_others"))
    t_idr = AC.do(lambda e: e.activation(identR[:], ident[:], ACT.Copy), x_in)

    s_wh, s_wl = sem("s_wh"), sem("s_wl")
    first = []
    marks, unit_done = [], []
    n_piece = [0]
    pieces = [4]
    side = []
    rate = [2]

    def unit(src, nk, ncol):
        n = len(unit_done)
        r, h, size = n % NR, n % NH, nk * ncol
        dst = raw[r][:, 0:size].rearrange("p (k c) -> p k c", k=nk)
        v = src.rearrange("(k p) c -> p k c", p=128)
        SP.dma(lambda e: e.dma_start(dst, v), s_raw[r], slot_split[n - NR] if n >= NR else None)
        loaded = (s_raw[r], 16 * (n // NR + 1))
        where = marks[n - LA] if n >= LA else first
        step = -(-nk // pieces[0])
        ready = [None] * nk
        for q, k0 in enumerate(range(0, nk, step)):
            pa, pd = where[q * 4 // pieces[0]]
            k1 = min(nk, k0 + step)
            c = slice(k0 * ncol, k1 * ncol)
            n_piece[0] += 1
            if q == 0:
                pa.wait(loaded, unit_done[n - NH] if n >= NH else None)
            pa.items.append(("run", lambda e, c=c: e.activation(wh[h][:, c], raw[r][:, c], ACT.Copy), s_wh, 1))
            pd.wait((s_wh, n_piece[0]))
            pd.items.append(("run", lambda e, c=c: e.tensor_tensor(
                wl[h][:, c], raw[r][:, c], wh[h][:, c].bitcast(F32), ALU.subtract), s_wl, 1))
            ready[k0:k1] = [(s_wl, n_piece[0])] * (k1 - k0)
        slot_split.append(ready[-1])
        unit_done.append(None)
        hi = wh[h][:, 0:size].rearrange("p (k c) -> p k c", k=nk)
        lo = wl[h][:, 0:size].rearrange("p (k c) -> p k c", k=nk)
        return n, hi, lo, ready
    slot_split = []

    def run_side(n):
        while n > 0 and side:
            side.pop(0)()
            n -= 1

    pair, ring, credit = [0], [(0, 2)], [0.0]
    cur = [0]

    def gemm(src, nk, c0, nch, xs, n0, n1, evac):
        pair[0] = (pair[0] + 1) % len(ring[0])
        b0 = cur[0] = ring[0][pair[0]]
        N = n1 - n0
        tk = [None] * nch
        while any(bank[b0 + m] is PENDING for m in range(nch)):
            run_side(1)
        for kg in range(0, nk, 8):
            g = min(8, nk - kg)
            n, hi, lo, ready = unit(src[kg * 128:(kg + g) * 128, c0:c0 + 128 * nch], g, 128 * nch)
            spots = [(AC.place(), DV.place())]
            if kg == 0:
                PE.wait(*[bank[b0 + m] for m in range(nch)])
            point = 0
            for part in range(2):
                for k in range(g):
                    if part == 0:
                        PE.wait(ready[k])
                    PE.wait(xs[kg + k][2 + part])
                    x = xs[kg + k][part][:, n0:n1]
                    for m in range(nch):
                        o = PS[b0 + m][:, 0:N]
                        a, b = hi[:, k, m * 128:(m + 1) * 128], lo[:, k, m * 128:(m + 1) * 128]
                        st = kg + k == 0 and part == 0
                        sp = kg + g == nk and k == g - 1 and part == 1
                        f = lambda e, o=o, a=a, x=x, st=st, sp=sp: e.matmul(o, a, x, start=st, stop=sp)
                        if part == 0:
                            PE.quiet(f)
                            PE.quiet(lambda e, o=o, a=b, x=x: e.matmul(o, a, x, start=False, stop=False))
                        elif sp or (k == g - 1 and m == nch - 1):
                            tk[m] = unit_done[n] = PE.do(f)
                        else:
                            PE.quiet(f)
                    point += 2 - part
                    if point < 3 * g:
                        while point * 4 // (3 * g) >= len(spots):
                            spots.append((AC.place(), DV.place()))
                        advance((2 - part) * 8 / g)
            marks.append(spots)
        free = evac([PS[b0 + m][:, 0:N] for m in range(nch)], tk)
        for m in range(nch):
            bank[b0 + m] = free[m]
        advance(1)

    def advance(share):
        if not side:
            credit[0] = 0.0
            return
        credit[0] += rate[0] * share / 24
        while credit[0] >= 1:
            credit[0] -= 1
            run_side(1)

    def drain():
        run_side(len(side) + 1000)

    def split(src, hi, lo, *after):
        a = AC.do(lambda e: e.activation(hi, src, ACT.Copy), *after)
        d = DV.do(lambda e: e.tensor_tensor(lo, src, hi.bitcast(F32), ALU.subtract), a, *after)
        return [a, d]

    def ln_exp():
        AC.quiet(lambda e: e.preload_act_table_set("natural_log_exp_and_others"))

    def ptr(o, i, rows):
        return lambda e: e.transpose(o, i, ident[0:rows, 0:rows])

    def copy_act(o, i, scale=1.0):
        return lambda e: e.activation(o, i, ACT.Copy, scale=scale)

    def fn_act(o, i, f, **kw):
        return lambda e: e.activation(o, i, f, **kw)

    def tt(o, a, b, op):
        return lambda e: e.tensor_tensor(o, a, b, op)

    def stt(o, a, s, b, op0, op1):
        return lambda e: e.scalar_tensor_tensor(out=o, in0=a, scalar=s, in1=b, op0=op0, op1=op1)

    def ts(o, a, s1, s2, op0, op1=None):
        if op1 is None:
            return lambda e: e.tensor_scalar(o, a, s1, None, op0)
        return lambda e: e.tensor_scalar(o, a, s1, s2, op0, op1)

    def mm(o, a, b, st=True, sp=True):
        return lambda e: e.matmul(o, a, b, start=st, stop=sp)

    def now():
        return [(q.sem, q.n) for q in (PE, AC, DV, GP) if q.n]

    xs = []
    h_t = [None] * KD
    for c in range(KD):
        b = 4 + c % 4
        f = slice(c * 128, (c + 1) * 128)
        PE.quiet(ptr(PS[b][:, 0:16], X0[:, f], 16), x_in, bank[b])
        PE.quiet(ptr(PS[b][:, 16:144], X1[:, f], 128))
        t = PE.do(ptr(PS[b][:, 144:272], X2[:, f], 128))
        s = split(PS[b][:, 0:T], XH[:, c, :], XL[:, c, :], t)
        bank[b] = s
        h_t[c] = GP.do(tt(H[:, c, :], XH[:, c, :].bitcast(F32), XL[:, c, :].bitcast(F32), ALU.add), s)
        xs.append((XH[:, c, :], XL[:, c, :], s[0], s[1]))
    first += [(AC.place(), DV.place())] * 4
    p_t = []
    prow_done = []

    def params(t):
        n = nrow[t]
        k = PE.do(ptr(PS[6][:, 0:n], prow[0:n, t, :], n), (s_p, n_p), bank[6])
        bank[6] = AC.do(copy_act(PV[:, t, 0:n], PS[6][:, 0:n]), k)
        p_t.append(bank[6])
        prow_done.append(k)
    for t in range(4):
        side.append(lambda t=t: params(t))
    credit[0] = -6.0
    fence = now()
    cstk.close()

    R = sb(b1, [128, KD, T])
    SQ = sb(b1, [128, 4, T])
    KXH = sb(b1, [128, KD, T], F32R)
    KXL = sb(b1, [128, KD, T], F32R)
    r_free = [list(fence) + [prow_done]]
    acc_t, last_t = [None], [None]

    def residual(j, n0):
        def evac(ps, tk):
            free = []
            for m in range(2):
                k = 2 * j + m
                t = DV.do(stt(R[:, k, n0:T], H[:, k, n0:T], ALPHA, ps[m], ALU.mult, ALU.add),
                          tk[m], h_t[k], r_free[0])
                free.append(t)

            last_t[0] = free
            for k in (2 * j, 2 * j + 1):
                if j == 3:
                    break
                if k == 1:
                    acc_t[0] = DV.do(tt(LNV[:, n0:T], R[:, 0, n0:T], R[:, 1, n0:T], ALU.add), free)
                elif k > 1:
                    acc_t[0] = DV.do(tt(LNV[:, n0:T], LNV[:, n0:T], R[:, k, n0:T], ALU.add), free, acc_t[0])
            return free
        return evac

    def rstd(psum, tk, eps, n):
        a = AC.do(fn_act(LNV[:, 0:n], psum, ACT.Ln, bias=cc[:, eps:eps + 1]), tk, m_c)
        return a, AC.do(fn_act(RS[:, 0:n], LNV[:, 0:n], ACT.Exp, scale=-0.5), a)

    def layer_norm(i, hi, lo, n0=0, spread=False):
        drain()
        res, d, a1, c_t, t = [], [None] * KD, [None] * KD, [None] * 4, {}
        mean, var = PS[7][:, n0:T], PS[6][:, n0:T]

        def means():
            ln_exp()
            PE.quiet(mm(mean, mean1[:], LNV[:, n0:T], True, False), acc_t[0], bank[7])
            PE.quiet(mm(mean, mean1[:], R[:, 6, n0:T], False, False), last_t[0][0])
            t["mean"] = PE.do(mm(mean, mean1[:], R[:, 7, n0:T], False, True), last_t[0][1])

        def centre(j):
            s = slice(2 * j, 2 * j + 2)
            m = mean.unsqueeze(1).to_broadcast([128, 2, T - n0])
            c_t[j] = DV.do(tt(XC[:, s, n0:T], R[:, s, n0:T], m, ALU.subtract), t["mean"], r_free[0])
            q = slice(2 * (j % 2), 2 * (j % 2) + 2)
            t["sq", j] = AC.do(fn_act(SQ[:, q, n0:T], XC[:, s, n0:T], ACT.Square), c_t[j], t.get(("var", j - 2)))
            bank[7] = c_t[j]

        def variance(j):
            for k in (2 * j, 2 * j + 1):
                f = mm(var, mean1[:], SQ[:, k % 4, n0:T], k == 0, k == KD - 1)
                t["var", j] = PE.do(f, t["sq", j], bank[6] if k == 0 else None)

        def root():
            bank[6], t["r"] = rstd(var, t["var", 3], 0, T - n0)

        def scale(k):
            d[k] = DV.do(tt(XC[:, k, n0:T], XC[:, k, n0:T], RS[:, 0:T - n0], ALU.mult), t["r"], c_t[k // 2])

        def high(k):
            g, b = pc("ln_gain", 8 * i + k), pc("ln_bias", 8 * i + k)
            a1[k] = AC.do(fn_act(hi[:, k, n0:T], XC[:, k, n0:T], ACT.Identity, scale=g, bias=b), d[k], p_t)

        def whole(k):
            g, b = pc("ln_gain", 8 * i + k), pc("ln_bias", 8 * i + k)
            h_t[k] = AC.do(fn_act(H[:, k, n0:T], XC[:, k, n0:T], ACT.Identity, scale=g, bias=b), d[k])
            if hi is not None:
                l = DV.do(tt(lo[:, k, n0:T], H[:, k, n0:T], hi[:, k, n0:T].bitcast(F32), ALU.subtract), h_t[k])
                res.append((hi[:, k, :], lo[:, k, :], a1[k], l))
            if k == KD - 1:
                r_free[0] = [c_t[-1], t["var", 3], h_t[k], l if hi is not None else None]
        steps = [means]
        for j in range(4):
            steps += [lambda j=j: centre(j), lambda j=j: variance(j)]
        steps += [root] + [lambda k=k: scale(k) for k in range(KD)]
        if hi is not None:
            steps += [lambda k=k: high(k) for k in range(KD)]
        steps += [lambda k=k: whole(k) for k in range(KD)]
        side.extend(steps)
        if not spread:
            drain()
        return res

    def ffn(wg, wu, wd, xs, n0=0):
        with ExitStack() as st:
            fence = now()
            HH, HL = sb(st, [128, KF, T], F32R), sb(st, [128, KF, T], F32R)
            SG = [sb(st, [128, 2, T]) for _ in range(2)]
            hid = []
            sg_t, hp_free = [None, None], [fence, fence]
            ring[0] = (0, 2, 4)
            for j in range(11):
                s = j % 2

                def evac_g(ps, tk):
                    sg_t[s] = [AC.do(fn_act(SG[s][:, m, n0:T], ps[m], ACT.Silu), tk[m], hp_free[s]) for m in range(2)]
                    return sg_t[s]

                def evac_u(ps, tk):
                    free = [DV.do(stt(SG[s][:, m, n0:T], SG[s][:, m, n0:T], 0.5, ps[m], ALU.mult, ALU.mult),
                                  tk[m], sg_t[s][m]) for m in range(2)]
                    hs = [split(SG[s][:, m, n0:T], HH[:, 2 * j + m, n0:T], HL[:, 2 * j + m, n0:T], free[m], fence)
                          for m in range(2)]
                    hp_free[s] = hs[0] + hs[1]
                    hid.extend((HH[:, 2 * j + m, :], HL[:, 2 * j + m, :], *hs[m]) for m in range(2))
                    return free
                gemm(wg, KD, 256 * j, 2, xs, n0, T, evac_g)
                gemm(wu, KD, 256 * j, 2, xs, n0, T, evac_u)
            drain()
            for j in range(4):
                gemm(wd, KF, 256 * j, 2, hid, n0, T, residual(j, n0))
            ring[0] = (0, 2)

    def short_conv(xs):
        with ExitStack() as st:
            fence = now()
            CH, CL = sb(st, [128, KD, T], F32R), sb(st, [128, KD, T], F32R)
            CT = [sb(st, [128, 2, T]) for _ in range(2)]
            Y = [sb(st, [128, 2, T]) for _ in range(2)]
            w_in = A["conv_w_in"][0]
            res = []
            u_free, y_free = [fence, fence], [fence, fence]
            ct, yt = [None], [None]
            for j in range(4):
                s = j % 2

                def evac_c(ps, tk):
                    ct[0] = [AC.do(copy_act(CT[s][:, m, :], ps[m]), tk[m], u_free[s]) for m in range(2)]
                    return ct[0]

                def evac_v(ps, tk):
                    u = [DV.do(tt(CT[s][:, m, :], CT[s][:, m, :], ps[m], ALU.mult), tk[m], ct[0][m]) for m in range(2)]
                    y = [DV.do(ts(Y[s][:, m, :], CT[s][:, m, :], pc("conv_w", 16 + 2 * j + m), None, ALU.mult),
                               u[m], p_t, y_free[s]) for m in range(2)]
                    for o in (1, 2):
                        y = [DV.do(stt(Y[s][:, m, o:T], CT[s][:, m, 0:T - o], pc("conv_w", 8 * (2 - o) + 2 * j + m),
                                       Y[s][:, m, o:T], ALU.mult, ALU.add), y[m]) for m in range(2)]
                    u_free[s] = y
                    yt[0] = y
                    return u

                def evac_b(ps, tk):
                    free = [DV.do(tt(Y[s][:, m, :], Y[s][:, m, :], ps[m], ALU.mult), tk[m], yt[0][m]) for m in range(2)]
                    hs = [split(Y[s][:, m, :], CH[:, 2 * j + m, :], CL[:, 2 * j + m, :], free[m], fence)
                          for m in range(2)]
                    y_free[s] = hs[0] + hs[1]
                    res.extend((CH[:, 2 * j + m, :], CL[:, 2 * j + m, :], *hs[m]) for m in range(2))
                    return free
                gemm(w_in, KD, 1024 + 256 * j, 2, xs, 0, T, evac_c)
                gemm(w_in, KD, 2048 + 256 * j, 2, xs, 0, T, evac_v)
                gemm(w_in, KD, 256 * j, 2, xs, 0, T, evac_b)
            for j in range(4):
                gemm(A["conv_w_out"][0], KD, 256 * j, 2, res, 0, T, residual(j, 0))

    ffn(A["ffn1_wg"][0], A["ffn1_wu"][0], A["ffn1_wd"][0], xs)
    xs = layer_norm(0, XH, XL)
    short_conv(xs)
    xs = layer_norm(1, XH, XL)
    ffn(A["ffn2_wg"][0], A["ffn2_wu"][0], A["ffn2_wd"][0], xs)
    kxs = layer_norm(2, KXH, KXL)

    fg = ExitStack()
    NCF = sb(fg, [128, T])
    NCH, NCL = sb(fg, [128, T], F32R), sb(fg, [128, T], F32R)
    CTT = sb(fg, [128, 3, 8])
    xf = XC[:, :, :].rearrange("p a c -> p (a c)")
    rf = R[:, :, :].rearrange("p a c -> p (a c)")
    CB = [xf[:, 0:528], xf[:, 528:1056]]
    Z8, L8 = xf[0:8, 1056:1328], xf[0:8, 1328:1600]
    XM, SMK = rf[0:16, 0:1024], rf[0:16, 1024:1024 + STRIP + MSTRIP]
    HOT = SQ[0:32, :, :].rearrange("p a c -> p (a c)")[:, 0:STRIP + MSTRIP]
    s_nc = []
    v = {}
    fence = now()
    GP.dma(lambda e: e.dma_start(XM, A["meta_tokens_2"]), s_b, fence)
    GP.dma(lambda e: e.dma_start(HOT, A["c_hot"]), s_b)
    GP.dma(lambda e: e.dma_start(SMK, A["c_smask"]), s_b)
    v["zero"] = [DV.do(lambda e, b=b: e.memset(b, 0.0), fence) for b in CB]

    def logits(k):
        v["t"] = PE.do(mm(PS[6][0:8, 0:T], WF[:, k, :], H[:, k, :], k == 0, k == KD - 1),
                       (s_f, 48), h_t[k], bank[6] if k == 0 else None)

    def logits_out():
        v["z"] = v["t"] = AC.do(fn_act(Z8, PS[6][0:8, 0:T], ACT.Identity, bias=FB[:, 0:1]), v["t"])
        bank[6] = v["z"]

    def softplus_steps(z, n, tmp, v):
        def s1():
            v["t"] = AC.do(fn_act(tmp, z, ACT.Abs), v["t"])

        def s2():
            v["t"] = AC.do(fn_act(tmp, tmp, ACT.Exp, scale=-1.0), v["t"])

        def s3():
            v["t"] = AC.do(fn_act(tmp, tmp, ACT.Ln, bias=cc[0:n, 2:3]), v["t"], m_c)
        return [s1, s2, s3]

    def log_gate():
        v["t"] = DV.do(stt(CB[0][0:8, 256:256 + T], Z8, 0.0, L8, ALU.min, ALU.subtract), v["t"], v["zero"])

    def cumsum_steps(bufs, n, v):
        def add(i, s):
            a, b = bufs[i], bufs[1 - i]
            v["t"] = DV.do(tt(b[0:n, 256:256 + T], a[0:n, 256:256 + T], a[0:n, 256 - s:256 - s + T], ALU.add), v["t"])
        return [lambda i=i: add(i % 2, 1 << i) for i in range(9)]
    C = CB[1][:, 256:256 + T]

    def gates_out():
        v["a"] = AC.do(fn_act(NCF[:], C, ACT.Copy, scale=-1.0), v["t"])

    def gates_split():
        s_nc.extend(split(NCF[:], NCH[:], NCL[:], v["a"]))

    def gates_T():
        for i, (q0, q1) in list(enumerate(QT))[1:]:
            k = PE.do(ptr(PS[6][0:q1 - q0, 8 * i:8 * i + 8], C[0:8, q0:q1], 8), v["t"], bank[6])
        bank[6] = AC.do(copy_act(CTT[:, 1:3, :], PS[6][:, 8:24].rearrange("p (a c) -> p a c", a=2)), k)
        s_nc.append(bank[6])

    def meta2():
        for k in range(KD):
            t = PE.do(ptr(PS[6][:, 16 * k:16 * k + 16], XM[:, k * 128:(k + 1) * 128], 16), (s_b, 48), bank[6])
        t = DV.do(lambda e: e.tensor_copy(H[:, :, 0:16], PS[6][:, 0:128].rearrange("p (k t) -> p k t", k=KD)),
                  t, v["z"])
        bank[6] = t
        h_t[:] = [[x, t] for x in h_t]
        r_free[0] = r_free[0] + [t] + s_nc

    WS = STRIP + MSTRIP
    sv = scratch

    def strips():
        k = PE.do(mm(PS[6][0:16, 0:STRIP], RB[:], HOT[:, 0:STRIP]), (s_b, 48), (s_f, 48), bank[6])
        k2 = PE.do(mm(PS[7][0:16, 0:MSTRIP], RB[:], HOT[:, STRIP:]), bank[7])
        d = DV.do(tt(SMK[:, 0:STRIP], SMK[:, 0:STRIP], PS[6][0:16, 0:STRIP], ALU.add), k)
        d2 = DV.do(tt(SMK[:, STRIP:], SMK[:, STRIP:], PS[7][0:16, 0:MSTRIP], ALU.add), k2)
        bank[6], bank[7] = d, d2
        GP.dma(lambda e: e.dma_start(sv.rearrange("q h j -> h q j"),
                                     SMK.unsqueeze(1).to_broadcast([16, 128, WS])), s_b, d, d2)
        r_free[0] = r_free[0] + [(s_b, 64)]
    side += [lambda k=k: logits(k) for k in range(KD)] + [logits_out]
    side += [ln_exp] + softplus_steps(Z8, 8, L8, v) + [log_gate] + cumsum_steps(CB, 8, v)
    side += [gates_out, gates_split, gates_T, meta2, strips]

    ffn(A["ffn1_wg"][1], A["ffn1_wu"][1], A["ffn1_wd"][1], kxs, NMETA)
    xs = layer_norm(3, XH, XL, NMETA, spread=True)

    def zero_pad(bufs, fence):
        return [DV.do(lambda e, b=b: e.memset(b[:], 0.0), fence) for b in bufs]

    class Softmax:

        def __init__(self, st, fence, tiles):
            self.tiles = tiles
            self.SS = [sb(st, [128, 432]) for _ in range(2)]
            self.P = [sb(st, [128, 432]) for _ in range(3)]
            self.PT0 = [sb(st, [128, T]) for _ in range(1)]
            self.PT1 = [sb(st, [128, 256]) for _ in range(1)]
            self.PT2 = [sb(st, [128, 128]) for _ in range(1)]
            self.MX = [sb(st, [128, 3]) for _ in range(2)]
            self.NM = [sb(st, [128, 3]) for _ in range(2)]
            self.SM = [sb(st, [128, 3]) for _ in range(2)]
            self.RC = [sb(st, [128, 3]) for _ in range(2)]
            self.init = zero_pad(self.MX + self.SM + self.PT0, fence)
            self.fence = fence
            self.p_free, self.s_free, self.pt_free = [None] * 3, [None] * 2, None
            self.p_t, self.ex_t = [None] * 3, [None] * 2

        COLS = ((416, 432), (272, 416), (0, 272))

        def reduce_exp(self, h, s_t, sink=None):
            i, P = h % 2, self.P[h % 3]
            SS, MX, NM, SM = (x[i] for x in (self.SS, self.MX, self.NM, self.SM))
            mx = []
            for q in self.tiles:
                c0, c1 = self.COLS[q]
                n = 16 if q == 0 else 128
                mx.append(DV.do(lambda e, c0=c0, c1=c1, n=n, q=q: e.tensor_reduce(
                    MX[0:n, q:q + 1], SS[0:n, c0:c1], AX.X, ALU.max), s_t[q], self.init))
            if sink is None:
                nm = DV.do(ts(NM[:], MX[:], -1.0, None, ALU.mult), mx)
            else:
                nm = DV.do(ts(NM[:], MX[:], sink, -1.0, ALU.max, ALU.mult), mx)
            ex = []
            for q in self.tiles:
                c0, c1 = self.COLS[q]
                n = 16 if q == 0 else 128
                ex.append(AC.do(fn_act(P[0:n, c0:c1], SS[0:n, c0:c1], ACT.Exp, bias=NM[0:n, q:q + 1],
                                       accum_out=SM[0:n, q:q + 1]), nm, self.p_free[h % 3], self.fence))
            self.s_free[i] = ex
            es = None
            if sink is not None:
                es = AC.do(fn_act(MX[:], NM[:], ACT.Exp, bias=sink), nm)
            self.ex_t[i] = ex, es

        def normalise(self, h):
            i, P = h % 2, self.P[h % 3]
            MX, SM, RC = (x[i] for x in (self.MX, self.SM, self.RC))
            ex, es = self.ex_t[i]
            if es is not None:
                ex = [DV.do(tt(SM[:], SM[:], MX[:], ALU.add), es, ex)]
            rc = [DV.do(lambda e: e.reciprocal(RC[:, 1:3], SM[:, 1:3]), ex, self.p_t[(h - 2) % 3])]
            if 0 in self.tiles:
                rc.append(DV.do(lambda e: e.reciprocal(RC[0:16, 0:1], SM[0:16, 0:1])))
            pt = []
            for q in self.tiles:
                c0, c1 = self.COLS[q]
                n = 16 if q == 0 else 128
                pt.append(GP.do(ts(P[0:n, c0:c1], P[0:n, c0:c1], RC[0:n, q:q + 1], None, ALU.mult), rc))
            self.p_t[h % 3] = pt

        def transposes(self, h):
            P = self.P[h % 3]
            PE.wait(self.p_t[h % 3], bank[6])
            t0 = 16
            if 0 in self.tiles:
                t0 = 0
                PE.quiet(ptr(PS[6][0:16, 0:16], P[0:16, 416:432], 16))
            PE.quiet(ptr(PS[6][0:16, 16:144], P[:, 272:288], 128))
            PE.quiet(ptr(PS[6][0:16, 144:272], P[:, 0:16], 128))
            k6 = PE.do(ptr(PS[6][:, 272:400], P[:, 144:272], 128))
            a0 = AC.do(copy_act(self.PT0[0][0:16, t0:272], PS[6][0:16, t0:272]), k6, self.pt_free, self.init)
            a2 = AC.do(copy_act(self.PT2[0][:], PS[6][:, 272:400]), k6)
            bank[6] = a2
            return [a0, a2]

        def transposes2(self, h):
            P = self.P[h % 3]
            PE.quiet(ptr(PS[7][:, 0:128], P[:, 288:416], 128), bank[7])
            k7 = PE.do(ptr(PS[7][:, 128:256], P[:, 16:144], 128))
            self.p_free[h % 3] = k7
            a1 = AC.do(copy_act(self.PT1[0][:], PS[7][:, 0:256]), k7, self.pt_free, self.fence)
            bank[7] = a1
            return [a1]

    def pipeline(h, a, n, b, b2, re, c, heads=8):
        r = []
        for step, x in ((a, h), (n, h - 1), (c, h - 3), (re, h), (b, h - 2), (b2, h - 2)):
            if 0 <= x < heads:
                r.append(lambda step=step, x=x: step(x))
        return r

    with ExitStack() as st:
        fence = now()
        OH, OL = sb(st, [128, KD, T], F32R), sb(st, [128, KD, T], F32R)
        QF, KF_, VF = ([sb(st, [128, 2, T]) for _ in range(2)] for _ in range(3))
        VM = [sb(st, [128, 3, 128]) for _ in range(4)]
        sm = Softmax(st, fence, (2, 1))
        vm_init = zero_pad(VM, fence)
        heads = {}
        ores = [None] * 8
        qkv_free = [fence, fence]

        def step_a(h):
            p, m, i = (h // 2) % 2, h % 2, h % 2
            q, k, v = QF[p][:, m, :], KF_[p][:, m, :], VF[p][:, m, :]
            inq = heads[h // 2]
            e_r = identR[:, h:h + 1].to_broadcast([128, 128])
            PE.wait(inq, bank[4], s_nc, t_idr)
            PE.quiet(mm(PS[4][:, 0:T], q[:, 144:272], k, True, False))
            PE.quiet(mm(PS[4][:, 0:T], e_r, NCH[:, :], False, False))
            k4 = PE.do(mm(PS[4][:, 0:T], e_r, NCL[:, :], False, True))
            PE.wait(bank[5])
            PE.quiet(mm(PS[5][:, 0:144], q[:, 16:144], k[:, 0:144], True, False))
            PE.quiet(mm(PS[5][:, 0:144], e_r, NCH[:, 0:144], False, False))
            k5 = PE.do(mm(PS[5][:, 0:144], e_r, NCL[:, 0:144], False, True))
            s2 = DV.do(stt(sm.SS[i][:, 0:272], PS[4][:, 0:T], CTT[:, 2, h:h + 1], cm[:], ALU.add, ALU.add),
                       k4, sm.s_free[i], fence, (s_c, 32))
            s1 = DV.do(stt(sm.SS[i][:, 272:416], PS[5][:, 0:144], CTT[:, 1, h:h + 1], cm[:, 128:272],
                           ALU.add, ALU.add), k5)
            bank[4], bank[5] = s2, s1
            PE.wait(bank[6])
            for t, (k0, k1) in enumerate(QT):
                kv = PE.do(ptr(PS[6][0:k1 - k0, 128 * t:128 * t + 128], v[:, k0:k1], 128))
            vf = heads.get(("vm", h - 4))
            a = AC.do(copy_act(VM[h % 4][0:16, 0, :], PS[6][0:16, 0:128]), kv, vf, vm_init)
            b = AC.do(copy_act(VM[h % 4][:, 1:3, :], PS[6][:, 128:384].rearrange("p (t c) -> p t c", t=2)), kv, vf)
            bank[6] = b
            heads[("v", h)] = [a, b]
            if m == 1:
                qkv_free[p] = [kv]
            heads[("s", h)] = [None, s1, s2]

        def step_re(h):
            sm.reduce_exp(h, heads[("s", h)])

        def step_b(h):
            heads[("pt", h)] = sm.transposes(h)

        def step_b2(h):
            heads[("pt", h)] += sm.transposes2(h)

        def step_c(h):
            i = h % 2
            PE.wait(heads[("pt", h)], heads[("v", h)], bank[7])
            PE.quiet(mm(PS[7][:, 16:T], VM[h % 4][:, 0, :], sm.PT0[0][:, 16:T], True, False))
            PE.quiet(mm(PS[7][:, 16:T], VM[h % 4][:, 1, :], sm.PT1[0][:], False, False))
            t = PE.do(mm(PS[7][:, 144:T], VM[h % 4][:, 2, :], sm.PT2[0][:], False, True))
            sm.pt_free = t
            heads[("vm", h)] = t
            s = split(PS[7][:, 16:T], OH[:, h, 16:T], OL[:, h, 16:T], t, fence)
            bank[7] = s
            ores[h] = (OH[:, h, :], OL[:, h, :], *s)

        def take(dst, p, scale, key, n0):
            def evac(ps, tk):
                t = [AC.do(copy_act(dst[p][:, m, n0:T], ps[m], scale), tk[m], qkv_free[p]) for m in range(2)]
                heads[key] = heads.get(key, []) + t
                return t
            return evac

        def kv(j):
            gemm(A["kv_w"], KD, 256 * j, 2, kxs, 0, T, take(KF_, j % 2, 1.0, j, 0))
            gemm(A["kv_w"], KD, 1024 + 256 * j, 2, kxs, 0, T, take(VF, j % 2, 1.0, j, 0))
        rate[0] = 24
        kv(0)
        drain()
        rate[0] = 6
        for j in range(4):
            p = j % 2
            if j:
                kv(j)
            gemm(A["attn_w_q"][0], KD, 256 * j, 2, xs, NMETA, T, take(QF, p, 1.0 / math.sqrt(128), j, NMETA))
            if j:
                drain()
            side.extend(x for h in (2 * j, 2 * j + 1) for x in pipeline(h, step_a, sm.normalise, step_b, step_b2, step_re, step_c))
        side.extend(pipeline(8, step_a, sm.normalise, step_b, step_b2, step_re, step_c))
        side.extend(pipeline(9, step_a, sm.normalise, step_b, step_b2, step_re, step_c))
        side.extend(pipeline(10, step_a, sm.normalise, step_b, step_b2, step_re, step_c))
        drain()
        rate[0] = 2
        for j in range(4):
            gemm(A["attn_w_o"][0], KD, 256 * j, 2, ores, NMETA, T, residual(j, NMETA))
    xs = layer_norm(4, XH, XL, NMETA)
    fg.close()
    ffn(A["ffn2_wg"][1], A["ffn2_wu"][1], A["ffn2_wd"][1], xs, NMETA)
    layer_norm(5, None, None, NMETA)
    fence = now()
    b1.close()

    b2 = ExitStack()
    u_stk = ExitStack()
    SQ2 = sb(u_stk, [128, 4, T])
    UT = sb(u_stk, [128, KD, T])

    def rms_norm(key, n0, fence, emit):
        n = T - n0
        var_t, free = None, [fence, fence]
        for j in range(4):
            q = slice(2 * (j % 2), 2 * (j % 2) + 2)
            a = AC.do(fn_act(SQ2[:, q, 0:n], H[:, 2 * j:2 * j + 2, n0:T], ACT.Square),
                      h_t[2 * j], h_t[2 * j + 1], free[j % 2])
            for k in (2 * j, 2 * j + 1):
                f = mm(PS[6][:, 0:n], mean1[:], SQ2[:, k % 4, 0:n], k == 0, k == KD - 1)
                var_t = PE.do(f, a, bank[6] if k == 0 else None)
            free[j % 2] = var_t
        a, r = rstd(PS[6][:, 0:n], var_t, 1, n)
        bank[6] = a
        d = []
        for k in range(KD):
            d.append(DV.do(tt(UT[:, k, 0:n], H[:, k, n0:T], RS[:, 0:n], ALU.mult), r, h_t[k], fence))
        emit([UT[:, k, 0:n] for k in range(KD)], d, [pc(key, k) for k in range(KD)])

    def normed(key, n0, fence):
        res = []

        def emit(u, d, w):
            hi = [XH[:, k, n0:T] for k in range(KD)]
            a = [AC.do(fn_act(hi[k], u[k], ACT.Copy, scale=w[k]), d[k], p_t) for k in range(KD)]
            for k in range(KD):
                l = DV.do(stt(XL[:, k, n0:T], u[k], w[k], hi[k].bitcast(F32), ALU.mult, ALU.subtract), a[k])
                res.append((XH[:, k, :], XL[:, k, :], a[k], l))
        rms_norm(key, n0, fence, emit)
        return res

    us = normed("norm_mix_w_2", 0, fence)
    W_IN = A["w_in_2"][0]
    u_stk.close()
    Z0, X_0, DT0, Q0, K0, GS0, GA0 = 0, 2048, 5120, 5152, 6176, 6432, 7456

    ma = ExitStack()
    GA = sb(ma, [128, KD, NV])
    ZS = sb(ma, [128, 16, NV])
    fence0 = now()
    with ExitStack() as st:
        fence = now()
        AH, AL = sb(st, [128, KD, NV], F32R), sb(st, [128, KD, NV], F32R)
        SNK = sb(st, [128, 16])
        B2 = sb(st, [128, 16, 272])
        B1 = sb(st, [128, 16, 16])
        B0 = sb(st, [16, 16, 16])
        QR = [sb(st, [128, T]) for _ in range(8)]
        KZ = [[sb(st, [128, T]) for _ in range(2)] for _ in range(2)]
        VV = sb(st, [128, T])
        VM = sb(st, [128, 3, 128])
        sm = Softmax(st, fence, (2, 1, 0))
        sk = A["attn_sinks_2"]
        GP.dma(lambda e: e.dma_start(SNK[:], bass.AP(tensor=sk.tensor, offset=sk.offset, ap=[[0, 128], [1, 16]])),
               s_b, fence)
        PT_ = 16 * WS

        def shifted(off, nq, n):
            return bass.AP(tensor=sv.tensor, offset=sv.offset + off, ap=[[PT_ - 1, nq], [WS, 16], [1, n]])
        GP.dma(lambda e: e.dma_start(B2[:, :, 16:272], shifted(127, 128, 256)), s_b, (s_b, 64))
        GP.dma(lambda e: e.dma_start(B2[:, :, 0:16], shifted(STRIP + 271 - 144, 128, 16)), s_b)
        GP.dma(lambda e: e.dma_start(B1[:], shifted(STRIP + 271 - 16, 128, 16)), s_b)
        GP.dma(lambda e: e.dma_start(B0[:], shifted(STRIP + 271, 16, 16)), s_b)
        bias_in = (s_b, 64 + 80)
        kz_init = zero_pad([KZ[0][0], KZ[0][1], KZ[1][0], KZ[1][1], VM], fence)
        q_t = [None] * 8
        kv_t = []
        ares = [None] * 8

        def evac_q(j):
            def evac(ps, tk):
                t = [AC.do(copy_act(QR[2 * j + m][:], ps[m], 0.125), tk[m], fence) for m in range(2)]
                q_t[2 * j], q_t[2 * j + 1] = t
                return t
            return evac

        def evac_kv(ps, tk):
            for g in range(2):
                for par in range(2):
                    o = KZ[par][g][64 * par:64 * par + 64, :]
                    kv_t.append(AC.do(copy_act(o, ps[0][64 * g:64 * g + 64, :]), tk[0], kz_init))
            v = DV.do(lambda e: e.tensor_copy(VV[:], ps[1]), tk[1], fence)

            def vt():
                PE.wait(v, bank[6])
                for t, (k0, k1) in enumerate(QT):
                    k = PE.do(ptr(PS[6][0:k1 - k0, 128 * t:128 * t + 128], VV[:, k0:k1], 128))
                a = AC.do(copy_act(VM[0:16, 0, :], PS[6][0:16, 0:128]), k, kz_init)
                b = AC.do(copy_act(VM[:, 1:3, :], PS[6][:, 128:384].rearrange("p (t c) -> p t c", t=2)), k)
                bank[6] = b
                kv_t.extend([a, b])
            side.append(vt)
            return [kv_t[3], v]

        pts = {}

        def swa_a(h):
            c, par, g, i = h // 2, h % 2, h // 8, h % 2
            q, kz = QR[c], KZ[par][g]
            PE.wait(q_t[c], kv_t, bank[4])
            k4 = PE.do(mm(PS[4][:, 0:T], q[:, 144:272], kz[:]))
            PE.wait(bank[5])
            PE.quiet(mm(PS[5][:, 0:144], q[:, 16:144], kz[:, 0:144]))
            k5 = PE.do(mm(PS[5][0:16, 144:160], q[:, 0:16], kz[:, 0:16]))
            SS = sm.SS[i]
            s2 = DV.do(tt(SS[:, 0:272], PS[4][:, 0:T], B2[:, h, :], ALU.add), k4, bias_in, sm.s_free[i], fence)
            DV.do(tt(SS[:, 272:288], PS[5][:, 0:16], B1[:, h, :], ALU.add), k5)
            s1 = DV.do(tt(SS[:, 288:416], PS[5][:, 16:144], B2[:, h, 144:272], ALU.add))
            s0 = DV.do(tt(SS[0:16, 416:432], PS[5][0:16, 144:160], B0[:, h, :], ALU.add))
            bank[4], bank[5] = s2, s0
            pts[("s", h)] = [s0, s1, s2]

        def swa_re(h):
            sm.reduce_exp(h, pts[("s", h)], SNK[:, h:h + 1])

        def swa_b(h):
            pts[h] = sm.transposes(h)

        def swa_b2(h):
            pts[h] += sm.transposes2(h)

        def swa_c(h):
            c, par, g, i = h // 2, h % 2, h // 8, h % 2
            PE.wait(pts[h], kv_t, bank[7])
            oo = PS[7][64 * par:64 * par + 64, :]
            gs = slice(64 * g, 64 * g + 64)
            PE.quiet(mm(oo[:, 0:T], VM[:, 0, gs], sm.PT0[0][:], True, False))
            PE.quiet(mm(oo[:, 16:T], VM[:, 1, gs], sm.PT1[0][:], False, False))
            t = PE.do(mm(oo[:, 144:T], VM[:, 2, gs], sm.PT2[0][:], False, True))
            sm.pt_free = t
            pp = slice(64 * par, 64 * par + 64)
            s = split(oo[:, TS:T], AH[pp, c, :], AL[pp, c, :], t, fence)
            bank[7] = s
            if par == 0:
                ares[c] = (AH[:, c, :], AL[:, c, :], *s)
            else:
                ares[c] = (ares[c][0], ares[c][1], [ares[c][2], s[0]], [ares[c][3], s[1]])

        def keep(dst, j, *after):
            def evac(ps, tk):
                return [AC.do(copy_act(dst[:, 2 * j + m, :], ps[m]), tk[m], *after) for m in range(2)]
            return evac

        gemm(W_IN, KD, K0, 2, us, 0, T, evac_kv)
        for j in range(4):
            gemm(W_IN, KD, Q0 + 256 * j, 2, us, 0, T, evac_q(j))
        drain()
        for h in range(19):
            side.extend(pipeline(h, swa_a, sm.normalise, swa_b, swa_b2, swa_re, swa_c, 16))
        rate[0] = 10
        for j in range(8):
            gemm(W_IN, KD, Z0 + 256 * j, 2, us, TS, T, keep(ZS, j, fence0))
        for j in range(4):
            gemm(W_IN, KD, GA0 + 256 * j, 2, us, TS, T, keep(GA, j, fence0))
        drain()
        rate[0] = 2
        last = (AC.sem, AC.n)
        g_t = [AC.do(fn_act(GA[:, k, :], GA[:, k, :], ACT.Sigmoid, bias=pc("gate_b_2", 8 + k)), last, p_t)
               for k in range(KD)]
        ga_t = [None] * KD
        z_t = [None] * 16

        def silu_z(k):
            z_t[k] = AC.do(fn_act(ZS[:, k, :], ZS[:, k, :], ACT.Silu), last)
        side += [lambda k=k: silu_z(k) for k in range(16)]
        rate[0] = 6

        def evac_ya(j):
            def evac(ps, tk):
                t = [DV.do(tt(GA[:, 2 * j + m, :], GA[:, 2 * j + m, :], ps[m], ALU.mult), tk[m], g_t[2 * j + m])
                     for m in range(2)]
                ga_t[2 * j:2 * j + 2] = t
                return t
            return evac
        for j in range(4):
            gemm(A["w_attn_branch_2"][0], KD, 256 * j, 2, ares, 0, NV, evac_ya(j))
        drain()

    Y = None
    ys = ExitStack()
    fence = now()
    YB = sb(ys, [128, 16, NV])
    y_t = [None] * 16
    with ExitStack() as st:
        BC = sb(st, [128, 8, T])
        CBM = sb(st, [128, 4, 432])
        ZD = sb(st, [32, T])
        LD = sb(st, [32, T])
        DTB, AL_, DC, DC2 = sb(st, [32, 1]), sb(st, [32, 1]), sb(st, [128, 16]), sb(st, [128, 32])
        CSB = [sb(st, [128, 256 + T]) for _ in range(2)]
        CSH, CSL = sb(st, [128, T], F32R), sb(st, [128, T], F32R)
        DTT, NCT = sb(st, [128, 3, 32]), sb(st, [128, 3, 32])
        CY = [sb(st, [128, 2, T]) for _ in range(2)]
        XDT = [sb(st, [128, 3, 128]) for _ in range(2)]
        EX = [sb(st, [128, 432]) for _ in range(4)]
        s_d = sem("s_d")
        GP.dma(lambda e: e.dma_start(DTB[:], A["ssd_dt_bias_2"].rearrange("l p -> p l")), s_d, fence)
        GP.dma(lambda e: e.dma_start(AL_[:], A["ssd_a_log_2"].rearrange("l p -> p l")), s_d)
        dd = A["ssd_d_2"]
        GP.dma(lambda e: e.dma_start(
            DC2[:], bass.AP(tensor=dd.tensor, offset=dd.offset, ap=[[0, 128], [1, 32]])), s_d)
        d_in = (s_d, 48)
        dc_t = [AC.do(copy_act(DC[64 * a:64 * a + 64, :],
                               DC2[64 * a:64 * a + 64, :].rearrange("p (c a) -> p c a", a=2)[:, :, a], 0.5), d_in, fence)
                for a in range(2)]
        cs_zero = zero_pad(CSB, fence)
        dt = {}
        w = {}

        def neg_a():
            a = AC.do(fn_act(AL_[:], AL_[:], ACT.Exp), d_in)
            w["a"] = DV.do(ts(AL_[:], AL_[:], -1.0, None, ALU.mult), a)

        def dt_done():
            w["dt"] = w["t"] = DV.do(stt(ZD[:], ZD[:], 0.0, LD[:], ALU.max, ALU.add), w["t"])

        def log_decay():
            w["t"] = DV.do(ts(CSB[0][0:32, 256:256 + T], ZD[:], AL_[:, 0:1], None, ALU.mult),
                           w["t"], w["a"], cs_zero)
        C = CSB[1][:, 256:256 + T]

        def decay_split():
            w["s"] = split(C, CSH[:], CSL[:], w["t"])

        def decay_T():
            PE.wait(bank[6], w["dt"], w["t"])
            for i, (t0, t1) in enumerate(ST):
                PE.quiet(ptr(PS[6][0:t1 - t0, 32 * i:32 * i + 32], ZD[:, t0:t1], 32))
                k = PE.do(ptr(PS[6][0:t1 - t0, 96 + 32 * i:128 + 32 * i], C[0:32, t0:t1], 32))
            r = []
            for o, dst, sc in ((0, DTT, 0.5), (96, NCT, -1.0)):
                r.append(AC.do(copy_act(dst[:, 0:2, :], PS[6][:, o:o + 64].rearrange("p (a c) -> p a c", a=2),
                                        sc), k, fence))
                r.append(AC.do(copy_act(dst[0:16, 2, :], PS[6][0:16, o + 64:o + 96], sc), k))
            bank[6] = r[-1]
            dt["t"] = r + w["s"]

        def evac_dt(ps, tk):
            z = w["t"] = AC.do(fn_act(ZD[:], ps[0][0:32, :], ACT.Identity, bias=DTB[:, 0:1]), tk[0], d_in, fence)
            ln_exp()
            side.extend(softplus_steps(ZD[:], 32, LD[:], w) + [dt_done, neg_a, log_decay]
                        + cumsum_steps(CSB, 32, w) + [decay_split, decay_T])
            return [z]

        TH = [sb(st, [128, 2, T]) for _ in range(2)]
        th_free, th_n = [fence] * 2, [0]

        def next_th():
            th_n[0] += 1
            return th_n[0] % 2

        def conv(ps, tk, c, dst, free):
            p = [pc("ssd_conv_w_2", 24 * 3 + c + m) for m in range(2)]
            y = [AC.do(fn_act(dst[m], ps[m], ACT.Identity, scale=p[m], bias=pc("ssd_conv_b_2", c + m)),
                       tk[m], p_t, free) for m in range(2)]
            for o in (1, 2, 3):
                y = [DV.do(stt(dst[m][:, o:T], ps[m][:, 0:T - o], pc("ssd_conv_w_2", 24 * (3 - o) + c + m),
                               dst[m][:, o:T], ALU.mult, ALU.add), y[m]) for m in range(2)]
            s = next_th()
            z = [AC.do(fn_act(TH[s][:, m, :], dst[m], ACT.Tanh, scale=0.5), y[m], th_free[s]) for m in range(2)]

            def finish(m):
                z[m] = th_free[s] = DV.do(stt(dst[m], TH[s][:, m, :], 1.0, dst[m], ALU.add, ALU.mult), z[m])
            finish(0)
            finish(1)
            return y, z

        gemm(W_IN, KD, DT0, 1, us, 0, T, evac_dt)
        rate[0] = 5
        bc_t = [None] * 8
        for j in range(4):
            def evac_bc(ps, tk):
                y, z = conv(ps, tk, 16 + 2 * j, [BC[:, 2 * j + m, :] for m in range(2)], fence)
                bc_t[2 * j:2 * j + 2] = z
                return y
            gemm(W_IN, KD, X_0 + 2048 + 256 * j, 2, us, 0, T, evac_bc)
        cb_t = [None] * 4

        def cb(g):
            b = 4 + g % 2
            B, C = BC[:, g, :], BC[:, 4 + g, :]
            PE.wait(bc_t[g], bc_t[4 + g], bank[b], bank[7])
            PE.quiet(mm(PS[b][:, 0:272], B[:, 0:128], C[:, :]))
            k1 = PE.do(mm(PS[b][:, 272:416], B[:, 128:256], C[:, 128:272]))
            k2 = PE.do(mm(PS[7][0:16, 0:16], B[:, 256:272], C[:, 256:272]))
            d = DV.do(stt(CBM[:, g, 0:416], PS[b][:, 0:416], 0.25, tri[:, 0:416], ALU.mult, ALU.mult), k1, fence, (s_c, 32))
            d2 = DV.do(stt(CBM[0:16, g, 416:432], PS[7][0:16, 0:16], 0.25, tri[0:16, 416:432], ALU.mult, ALU.mult), k2)
            bank[b], bank[7] = d, d2
            cb_t[g] = [d, d2]
        for g in range(4):
            side.append(lambda g=g: cb(g))
        xdt_free, xs_free = [fence, fence], [fence, fence]
        ex_free, m_free = [None] * 4, [None] * 4
        xs_t, m_t, xd_t, e_t = {}, {}, {}, {}

        def ssd_x(c):
            p = c % 2
            x = CY[(c // 2) % 2][:, c % 2, :]
            PE.wait(bank[6], xs_t[c])
            for i, (t0, t1) in enumerate(ST):
                k = PE.do(ptr(PS[6][0:t1 - t0, 128 * i:128 * i + 128], x[:, t0:t1], 128))
            o = XDT[p][:, 0:2, :].rearrange("p t (h d) -> p t h d", h=2)
            src = PS[6][:, 0:256].rearrange("p (t h d) -> p t h d", t=2, h=2)
            d = DV.do(tt(o, src, DTT[:, 0:2, 2 * c:2 * c + 2].unsqueeze(3).to_broadcast([128, 2, 2, 64]), ALU.mult),
                      k, dt["t"], xdt_free[p])
            o2 = XDT[p][0:16, 2, :].rearrange("p (h d) -> p h d", h=2)
            s2 = PS[6][0:16, 256:384].rearrange("p (h d) -> p h d", h=2)
            d2 = DV.do(tt(o2, s2, DTT[0:16, 2, 2 * c:2 * c + 2].unsqueeze(2).to_broadcast([16, 2, 64]), ALU.mult), k)
            bank[6] = d2
            xd_t[c] = [d, d2]

        def ssd_e(h):
            b, i = 4 + h % 2, h % 4
            e_r = identR[:, h:h + 1].to_broadcast([128, 128])
            PE.wait(bank[b], dt["t"], t_idr)
            PE.quiet(mm(PS[b][:, 0:T], e_r, CSH[:, :], True, False))
            k = PE.do(mm(PS[b][:, 0:T], e_r, CSL[:, :], False, True))
            E = EX[i]
            DV.do(ts(E[:, 0:272], PS[b][:, 0:T], NCT[:, 0, h:h + 1], 0.0, ALU.add, ALU.min),
                  k, dt["t"], m_free[i], fence)
            c1 = DV.do(ts(E[:, 272:416], PS[b][:, 128:T], NCT[:, 1, h:h + 1], 0.0, ALU.add, ALU.min))
            c2 = DV.do(ts(E[0:16, 416:432], PS[b][0:16, 256:T], NCT[0:16, 2, h:h + 1], 0.0, ALU.add, ALU.min))
            bank[b] = c2
            e_t[h] = [AC.do(fn_act(E[:, 0:416], E[:, 0:416], ACT.Exp), c1),
                      AC.do(fn_act(E[0:16, 416:432], E[0:16, 416:432], ACT.Exp), c2)]

        def ssd_m(h):
            E, g = EX[h % 4], h // 8
            m_t[h] = [GP.do(tt(E[:, 0:416], E[:, 0:416], CBM[:, g, 0:416], ALU.mult), e_t[h], cb_t[g]),
                      GP.do(tt(E[0:16, 416:432], E[0:16, 416:432], CBM[0:16, g, 416:432], ALU.mult))]

        def ssd_y(c):
            p = c % 2
            PE.wait(bank[7], xd_t[c])
            for par in range(2):
                h = 2 * c + par
                M = EX[h % 4]
                o = PS[7][64 * par:64 * par + 64, :]
                hs = slice(64 * par, 64 * par + 64)
                PE.wait(m_t[h])
                PE.quiet(mm(o[:, 0:T], XDT[p][:, 0, hs], M[:, 0:272], True, False))
                PE.quiet(mm(o[:, 128:T], XDT[p][:, 1, hs], M[:, 272:416], False, False))
                k = PE.do(mm(o[:, 256:T], XDT[p][0:16, 2, hs], M[0:16, 416:432], False, True))
                m_free[h % 4] = k
            xdt_free[p] = k
            x = CY[(c // 2) % 2][:, c % 2, TS:T]
            d = DV.do(stt(YB[:, c, :], x, DC[:, c:c + 1], PS[7][:, TS:T], ALU.mult, ALU.add), k, dc_t, fence)
            bank[7] = d
            xs_free[(c // 2) % 2] = [d]
            y_t[c] = GP.do(tt(YB[:, c, :], YB[:, c, :], ZS[:, c, :], ALU.mult), d, z_t[c])

        credit[0] = -4.0
        rate[0] = 12
        for j in range(8):
            def evac_xs(ps, tk):
                s = j % 2
                y, z = conv(ps, tk, 2 * j, [CY[s][:, m, :] for m in range(2)], xs_free[s])
                xs_t[2 * j], xs_t[2 * j + 1] = z
                return y
            gemm(W_IN, KD, X_0 + 256 * j, 2, us, 0, T, evac_xs)
            drain()
            for c in (2 * j, 2 * j + 1):
                if c > 1:
                    side.append(lambda c=c: ssd_y(c - 2))
                side += [lambda c=c: ssd_x(c), lambda c=c: ssd_e(2 * c), lambda c=c: ssd_e(2 * c + 1),
                         lambda c=c: ssd_m(2 * c), lambda c=c: ssd_m(2 * c + 1)]
        side += [lambda: ssd_y(14), lambda: ssd_y(15)]
        drain()
        rate[0] = 2
        fence = now()
    fin = ExitStack()
    YH, YL = sb(fin, [128, 16, NV], F32R), sb(fin, [128, 16, NV], F32R)
    SY = sb(fin, [128, 4, NV])
    GS = sb(fin, [128, KD, NV])
    gs_t = [None] * KD
    yres = []

    gn = {}

    def gn_sum(g):
        s = slice(4 * g, 4 * g + 4)
        a = AC.do(fn_act(SY[:], YB[:, s, :], ACT.Square), y_t[4 * g:4 * g + 4], fence, gn.get("sy"))
        PE.wait(a, bank[6])
        for k in range(4):
            t = PE.do(mm(PS[6][:, 0:NV], mean5[:], SY[:, k, :], k == 0, k == 3))
        gn["sy"] = t
        gn[g] = t

    def gn_rstd(g):
        s = slice(4 * g, 4 * g + 4)
        a, r = rstd(PS[6][:, 0:NV], gn[g], 1, NV)
        bank[6] = a
        rb = RS[:, 0:NV].unsqueeze(1).to_broadcast([128, 4, NV])
        gn[g] = DV.do(tt(YB[:, s, :], YB[:, s, :], rb, ALU.mult), r)

    def gn_out(k):
        w = pc("ssd_norm_w_2", k)
        a = AC.do(fn_act(YH[:, k, :], YB[:, k, :], ACT.Copy, scale=w), gn[k // 4])
        l = DV.do(stt(YL[:, k, :], YB[:, k, :], w, YH[:, k, :].bitcast(F32), ALU.mult, ALU.subtract), a)
        yres.append((YH[:, k, :], YL[:, k, :], a, l))
    for g in range(4):
        side.append(lambda g=g: gn_sum(g))
        side.append(lambda g=g: gn_rstd(g))
        side += [lambda k=k: gn_out(k) for k in range(4 * g, 4 * g + 4)]
    rate[0] = 8
    last = now()
    warm = [ln_exp()]
    for j in range(4):
        def evac_gs(ps, tk):
            t = [AC.do(copy_act(GS[:, 2 * j + m, :], ps[m]), tk[m], fence) for m in range(2)]
            gs_t[2 * j:2 * j + 2] = t
            return t
        gemm(W_IN, KD, GS0 + 256 * j, 2, us, TS, T, evac_gs)
    drain()
    rate[0] = 2
    for k in range(KD):
        gs_t[k] = AC.do(fn_act(GS[:, k, :], GS[:, k, :], ACT.Sigmoid, bias=pc("gate_b_2", k)), gs_t[k])
    x_free = now()
    mres = []
    for j in range(4):
        def evac_ys(ps, tk):
            t = [DV.do(tt(GS[:, 2 * j + m, :], GS[:, 2 * j + m, :], ps[m], ALU.mult), tk[m], gs_t[2 * j + m])
                 for m in range(2)]
            for m in range(2):
                k = 2 * j + m
                d = DV.do(tt(GS[:, k, :], GS[:, k, :], GA[:, k, :], ALU.add), t[m], ga_t[k])
                s = split(GS[:, k, :], XH[:, k, TS:T], XL[:, k, TS:T], d, x_free)
                mres.append((XH[:, k, :], XL[:, k, :], *s))
            return t
        gemm(A["w_ssd_branch_2"][0], 16, 256 * j, 2, yres, 0, NV, evac_ys)

    def add_h(j, n0):
        def evac(ps, tk):
            t = [DV.do(tt(H[:, 2 * j + m, n0:T], H[:, 2 * j + m, n0:T], ps[m], ALU.add), tk[m], h_t[2 * j + m])
                 for m in range(2)]
            h_t[2 * j:2 * j + 2] = t
            return t
        return evac
    for j in range(4):
        gemm(A["w_out_2"][0], KD, 256 * j, 2, mres, TS, T, add_h(j, TS))
    fence = now()
    fin.close()
    ys.close()
    ma.close()

    SQ2 = sb(b2, [128, 4, T])
    UT = sb(b2, [128, KD, T])
    us = normed("norm_ffn_w_2", TS, fence)
    NO = T - NMETA
    with ExitStack() as st:
        HH, HL = sb(st, [128, KF, NO], F32R), sb(st, [128, KF, NO], F32R)
        OT = sb(st, [128, 2, D])
        FN = sb(st, [128, 4, NO])
        SQF = sb(st, [128, 3, NO])
        UP = [sb(st, [128, 2, NO]) for _ in range(2)]
        GT = [sb(st, [128, 2, NO]) for _ in range(2)]
        free = [fence, fence]
        hid, up_t = [], [None]
        ring[0] = (0, 2, 4)

        def fw(tap, c):
            return pc("fw01", 44 * tap + c) if tap < 2 else pc("fw2", c)

        def conv3(ps, tk, c, dst, free):
            y = [AC.do(fn_act(dst[:, m, :], ps[m][:, 2:2 + NO], ACT.Identity, scale=fw(2, c + m),
                              bias=pc("ffn_conv_b_2", c + m)), tk[m], free) for m in range(2)]
            for o in (1, 0):
                y = [DV.do(stt(dst[:, m, :], ps[m][:, o:o + NO], fw(o, c + m), dst[:, m, :], ALU.mult, ALU.add),
                           y[m]) for m in range(2)]
            return y
        for j in range(11):
            s = j % 2

            def evac_g(ps, tk):
                y = conv3(ps, tk, 22 + 2 * j, GT[s], free[s])
                up_t[0] = [AC.do(fn_act(GT[s][:, m, :], GT[s][:, m, :], ACT.Silu), y[m]) for m in range(2)]
                return y

            def evac_u(ps, tk):
                y = conv3(ps, tk, 2 * j, UP[s], free[s])
                d = [DV.do(tt(UP[s][:, m, :], UP[s][:, m, :], GT[s][:, m, :], ALU.mult), y[m], up_t[0][m])
                     for m in range(2)]
                hs = [split(UP[s][:, m, :], HH[:, 2 * j + m, :], HL[:, 2 * j + m, :], d[m], fence) for m in range(2)]
                free[s] = hs[0] + hs[1]
                hid.extend((HH[:, 2 * j + m, :], HL[:, 2 * j + m, :], *hs[m]) for m in range(2))
                return y
            gemm(A["w_ffn_in_2"][0], KD, FF + 256 * j, 2, us, TS, T, evac_g)
            gemm(A["w_ffn_in_2"][0], KD, 256 * j, 2, us, TS, T, evac_u)
        drain()
        ring[0] = (0, 2)
        rate[0] = 8
        warm.append(ln_exp())
        fn_free, sq_free, sq_t, tr = [None] * 4, [None] * 3, [None] * KD, [None] * 4
        acc = [None]

        def last_T(k):
            i, b = k % 4, 4 + k // 2
            a = AC.do(fn_act(FN[:, i, :], H[:, k, NMETA:T], ACT.Copy, scale=pc("norm_final_w_2", k)),
                      h_t[k], fn_free[i], fence)
            PE.wait(a, bank[b] if k % 2 == 0 else None)
            for t in range(2):
                c0 = 256 * t + 128 * (k % 2)
                fn_free[i] = tr[k // 2] = PE.do(ptr(PS[b][:, c0:c0 + 128], FN[:, i, 128 * t:128 * t + 128], 128))

        def last_sq(k):
            i = 1 + k % 2 if k else 0
            sq_t[k] = AC.do(fn_act(SQF[:, i, :], H[:, k, NMETA:T], ACT.Square), h_t[k], sq_free[i], fence)
            if k == 0:
                acc[0] = sq_t[k]
            elif k < 6:
                acc[0] = sq_free[i] = GP.do(tt(SQF[:, 0, :], SQF[:, 0, :], SQF[:, i, :], ALU.add), sq_t[k], acc[0])

        def add_last(j):
            def evac(ps, tk):
                free = add_h(j, NMETA)(ps, tk)
                for k in (2 * j, 2 * j + 1):
                    side.extend([lambda k=k: last_sq(k), lambda k=k: last_T(k)])
                return free
            return evac
        for j in range(4):
            gemm(A["w_ffn_out_2"][0], KF, 256 * j, 2, hid, 0, NO, add_last(j))

        drain()
        bs = 2 - cur[0]
        for t in range(2):
            q = slice(128 * t, 128 * t + 128)
            PE.wait(bank[bs])
            PE.quiet(mm(PS[bs][:, t:t + 1], SQF[:, 0, q], mean1[:, 0:1], True, False), acc[0])
            PE.quiet(mm(PS[bs][:, t:t + 1], SQF[:, 1, q], mean1[:, 0:1], False, False), sq_t[6])
            k = PE.do(mm(PS[bs][:, t:t + 1], SQF[:, 2, q], mean1[:, 0:1], False, True), sq_t[7])
        r = AC.do(fn_act(LNV[:, 0:2], PS[bs][:, 0:2], ACT.Ln, bias=cc[:, 1:2]), k)
        r = AC.do(fn_act(RS[:, 0:2], LNV[:, 0:2], ACT.Exp, scale=-0.5), r)
        s_out = sem("s_out")
        for b in range(4):
            o = []
            for t in range(2):
                src, dst = PS[4 + b][:, 256 * t:256 * t + 256], OT[:, t, 256 * b:256 * b + 256]
                if b % 2:
                    o.append(AC.do(fn_act(dst, src, ACT.Copy, scale=RS[:, t:t + 1]), r, tr[b], fence))
                else:
                    o.append(DV.do(ts(dst, src, RS[:, t:t + 1], None, ALU.mult), r, tr[b], fence))
            SP.dma(lambda e, b=b: e.dma_start(
                out[0].rearrange("(t p) c -> p t c", p=128)[:, :, 256 * b:256 * b + 256],
                OT[:, :, 256 * b:256 * b + 256]), s_out, o)
        SP.wait((s_out, 64))
    b2.close()

    block = ctx.enter_context(nc.Block())

    @block.sync
    def _(e):
        SP.run(e)

    @block.gpsimd
    def _(e):
        GP.run(e)

    @block.scalar
    def _(e):
        AC.run(e)

    @block.vector
    def _(e):
        DV.run(e)

    @block.tensor
    def _(e):
        PE.run(e)


def kernel(**inputs):
    import concourse.bacc as bacc
    from concourse.bass_utils import run_bass_kernel_spmd

    nc = bacc.Bacc("TRN2", target_bir_lowering=False, num_devices=1)
    arrays = {n: np.ascontiguousarray(a) for n, a in inputs.items()}
    arrays.update(constants())
    arrays = {f"in_{n}": a for n, a in arrays.items()}
    A = {n[3:]: nc.dram_tensor(n, a.shape, mybir.dt.from_np(a.dtype), kind="ExternalInput").ap()
         for n, a in arrays.items()}
    out = nc.dram_tensor("out_y", (1, 256, 1024), F32, kind="ExternalOutput").ap()
    scratch = nc.dram_tensor("strips", (128, 16, STRIP + MSTRIP), F32, kind="Internal").ap()
    program(nc, A, out, scratch)
    r = run_bass_kernel_spmd(nc, [arrays], core_ids=[0])
    return r.results[0]["out_y"]
```
